# Optimizing a Trainium2 kernel written in Bass

```python
import jax, jax.numpy as jnp
from jax import lax
import numpy as np

D_MODEL = 1024
BATCH = 1
SEQ = 1024
DEPTH = 1
DEC_BATCH = 1
DEC_SEQ = 64
PAST_LEN = 1024

CHUNK = 64
HEAD_DIM = 64
N_HEADS = (D_MODEL // 2) // HEAD_DIM
ATT_DIM = N_HEADS * HEAD_DIM
CONV_DIM = D_MODEL // 2
CONV_W = 3
MIX_DIM = ATT_DIM + CONV_DIM
IN_DIM = 4 * ATT_DIM + N_HEADS + 4 * CONV_DIM
SPLIT_POINTS = (ATT_DIM, 2 * ATT_DIM, 3 * ATT_DIM, 4 * ATT_DIM, 4 * ATT_DIM + N_HEADS,
                4 * ATT_DIM + N_HEADS + CONV_DIM, 4 * ATT_DIM + N_HEADS + 2 * CONV_DIM,
                4 * ATT_DIM + N_HEADS + 3 * CONV_DIM)
Q_BLOCK = 128
ATTN_SCALE = HEAD_DIM ** -0.5
EPS = 1e-6
NEG = -1e30

kernel_name = "fox_shortconv_parallel_hybrid_step"

def rmsnorm(x, g):
    xf = x.astype(jnp.float32)
    y = xf * lax.rsqrt(jnp.mean(xf * xf, axis=-1, keepdims=True) + EPS)
    return (y * g.astype(jnp.float32)).astype(x.dtype)

def fox_attention(q, k, v, c_q, c_k, q_pos, k_pos):
    s = jnp.einsum('bqhd,bkhd->bhqk', q, k, preferred_element_type=jnp.float32) * ATTN_SCALE
    decay = jnp.transpose(c_q, (0, 2, 1))[..., :, None] - jnp.transpose(c_k, (0, 2, 1))[..., None, :]
    s = jnp.where(k_pos[None, :] <= q_pos[:, None], s + decay, NEG)
    p = jax.nn.softmax(s, axis=-1)
    return jnp.einsum('bhqk,bkhd->bqhd', p.astype(v.dtype), v)

def mixer_layer(x, norm_g, w_in, b_f, q_g, k_g, conv_w, att_g, conv_g, w_out,
                past_k=None, past_v=None, past_logf=None, past_conv=None):
    b, n, _ = x.shape
    h = rmsnorm(x, norm_g)
    proj = h @ w_in
    q, k, v, g_a, f_pre, cb, cc, ch, g_c = jnp.split(proj, SPLIT_POINTS, axis=-1)
    q = rmsnorm(q.reshape(b, n, N_HEADS, HEAD_DIM), q_g)
    k = rmsnorm(k.reshape(b, n, N_HEADS, HEAD_DIM), k_g)
    v = v.reshape(b, n, N_HEADS, HEAD_DIM)
    logf = jax.nn.log_sigmoid((f_pre + b_f).astype(jnp.float32))

    if past_k is None:
        c = jnp.cumsum(logf, axis=1)
        outs = []
        for i in range(n // Q_BLOCK):
            s0, e = i * Q_BLOCK, (i + 1) * Q_BLOCK
            outs.append(fox_attention(q[:, s0:e], k[:, :e], v[:, :e], c[:, s0:e], c[:, :e],
                                      jnp.arange(s0, e), jnp.arange(e)))
        att = jnp.concatenate(outs, axis=1)
        conv_past = jnp.zeros((b, CONV_W - 1, CONV_DIM), x.dtype)
    else:
        p_len = past_k.shape[1]
        k_all = jnp.concatenate([past_k.astype(k.dtype), k], axis=1)
        v_all = jnp.concatenate([past_v.astype(v.dtype), v], axis=1)
        c = jnp.cumsum(jnp.concatenate([past_logf.astype(jnp.float32), logf], axis=1), axis=1)
        att = fox_attention(q, k_all, v_all, c[:, p_len:], c,
                            p_len + jnp.arange(n), jnp.arange(p_len + n))
        conv_past = past_conv.astype(x.dtype)

    u = cc * ch
    u_pad = jnp.concatenate([conv_past, u], axis=1)
    y = sum(conv_w[i] * u_pad[:, i:i + n] for i in range(CONV_W))
    z = cb * y

    att = att.reshape(b, n, ATT_DIM)
    mix = jnp.concatenate([rmsnorm(att, att_g) * jax.nn.silu(g_a),
                           rmsnorm(z, conv_g) * jax.nn.silu(g_c)], axis=-1)
    out = x + mix @ w_out
    return out, k, v, logf.astype(x.dtype), u_pad[:, -(CONV_W - 1):]

def setup_inputs(seed: int = 0) -> dict:
    key = jax.random.key(seed)
    ks = jax.random.split(key, 16)
    f32 = jnp.float32
    x_prompt = jax.random.normal(ks[0], (BATCH, SEQ, D_MODEL), f32)
    x_sample = jax.random.normal(ks[1], (DEC_BATCH, DEC_SEQ, D_MODEL), f32)
    cache_k = jax.random.normal(ks[2], (DEPTH, DEC_BATCH, PAST_LEN, N_HEADS, HEAD_DIM), f32)
    cache_v = jax.random.normal(ks[3], (DEPTH, DEC_BATCH, PAST_LEN, N_HEADS, HEAD_DIM), f32)
    cache_logf = jax.nn.log_sigmoid(3.0 + jax.random.normal(ks[4], (DEPTH, DEC_BATCH, PAST_LEN, N_HEADS), f32))
    state_conv = 0.5 * jax.random.normal(ks[5], (DEPTH, DEC_BATCH, CONV_W - 1, CONV_DIM), f32)
    norm_g = 1.0 + 0.01 * jax.random.normal(ks[6], (DEPTH, D_MODEL), f32)
    w_in = jax.random.normal(ks[7], (DEPTH, D_MODEL, IN_DIM), f32) * D_MODEL ** -0.5
    b_f = jax.random.uniform(ks[8], (DEPTH, N_HEADS), f32, minval=1.0, maxval=6.0)
    q_norm_g = 1.0 + 0.01 * jax.random.normal(ks[9], (DEPTH, HEAD_DIM), f32)
    k_norm_g = 1.0 + 0.01 * jax.random.normal(ks[10], (DEPTH, HEAD_DIM), f32)
    conv_w = jax.random.normal(ks[11], (DEPTH, CONV_W, CONV_DIM), f32) * CONV_W ** -0.5
    att_out_g = 1.0 + 0.01 * jax.random.normal(ks[12], (DEPTH, ATT_DIM), f32)
    conv_out_g = 1.0 + 0.01 * jax.random.normal(ks[13], (DEPTH, CONV_DIM), f32)
    w_out = jax.random.normal(ks[14], (DEPTH, MIX_DIM, D_MODEL), f32) * (0.5 * MIX_DIM ** -0.5)
    return {"x_prompt": x_prompt, "x_sample": x_sample, "cache_k": cache_k, "cache_v": cache_v,
            "cache_logf": cache_logf, "state_conv": state_conv, "norm_g": norm_g, "w_in": w_in,
            "b_f": b_f, "q_norm_g": q_norm_g, "k_norm_g": k_norm_g, "conv_w": conv_w,
            "att_out_g": att_out_g, "conv_out_g": conv_out_g, "w_out": w_out}

def reference(x_prompt, x_sample, cache_k, cache_v, cache_logf, state_conv, norm_g, w_in, b_f,
              q_norm_g, k_norm_g, conv_w, att_out_g, conv_out_g, w_out):
    yp, ys = x_prompt, x_sample
    kp, vp, fp, cp, ksm, vsm, fsm, csm = [], [], [], [], [], [], [], []
    for l in range(DEPTH):
        params = (norm_g[l], w_in[l], b_f[l], q_norm_g[l], k_norm_g[l], conv_w[l],
                  att_out_g[l], conv_out_g[l], w_out[l])
        yp, k1, v1, f1, c1 = mixer_layer(yp, *params)
        ys, k2, v2, f2, c2 = mixer_layer(ys, *params, cache_k[l], cache_v[l], cache_logf[l], state_conv[l])
        kp.append(k1); vp.append(v1); fp.append(f1); cp.append(c1)
        ksm.append(k2); vsm.append(v2); fsm.append(f2); csm.append(c2)
    return (yp, ys, jnp.stack(kp), jnp.stack(vp), jnp.stack(fp), jnp.stack(cp),
            jnp.stack(ksm), jnp.stack(vsm), jnp.stack(fsm), jnp.stack(csm))


_drawn_inputs = setup_inputs


def setup_inputs(seed=0):
    import zlib

    import numpy as np

    out = dict(_drawn_inputs(seed))
    spreads = {}
    factors = {'cache_logf': 27.115,
     'state_conv': 9.285,
     'norm_g': 3.817,
     'q_norm_g': 8.0,
     'k_norm_g': 5.107,
     'att_out_g': 64.0,
     'conv_out_g': 64.0}
    for name, (base, spread) in spreads.items():
        noise = np.random.default_rng([zlib.crc32(name.encode()), seed]).standard_normal(out[name].shape)
        drawn = base * np.exp(spread * noise) if base else spread * noise
        out[name] = __import__('jax').numpy.asarray(drawn.astype(out[name].dtype))
    for name, factor in factors.items():
        out[name] = (out[name] * factor).astype(out[name].dtype)
    return out
```

```python
from contextlib import ExitStack

import concourse.bass as bass
from concourse import mybir

ALU = mybir.AluOpType
ACT = mybir.ActivationFunctionType
AX = mybir.AxisListType.X
F32 = mybir.dt.float32
F32R = mybir.dt.float32r
BF16 = mybir.dt.bfloat16

P = 128
DM = 1024
KD = DM // P
NH = 8
HD = 64
AD = NH * HD
CD = 512
CJ = CD // P
SEQ = 1024
NS = 64
PAST = 1024
TOK = SEQ + NS
NT = 9
PB = SEQ // P
NB = 2 * PB + 1
NEW = PB
EPS = 1e-6
CUTS = [(0, 384), (384, 384), (768, 320)]
COL_F = 4 * AD
COL_B, COL_C, COL_H, COL_G = (COL_F + NH + i * CD for i in range(4))


def rows(i):
    return P if i < PB else NS


def build(nc, x_prompt, x_sample, cache_k, cache_v, cache_logf, state_conv, norm_g, w_in, b_f,
          q_norm_g, k_norm_g, conv_w, att_out_g, conv_out_g, w_out, eye, future, upto,
          y_prompt, y_sample, k_prompt, v_prompt, logf_prompt, k_sample, v_sample, logf_sample,
          conv_last):
    ctx = ExitStack()
    with ctx:
        at = [16512]

        def keep(name, shape, dt):
            size = 2 if dt == BF16 else 4
            for n in shape[1:]:
                size *= n
            t = nc.alloc_sbuf_tensor_at(name, shape, dt, offset=at[0])
            at[0] += (size + 31) // 32 * 32
            return t

        ident = keep("ident", [P, P], F32)
        ident_r = keep("ident_r", [P, P], F32R)
        ident_b = keep("ident_b", [P, P], BF16)
        future_b = keep("future_b", [P, P], BF16)
        upto_f = keep("upto_f", [P, P], F32)
        ones_f = keep("ones_f", [P, P], F32)
        eps_c = keep("eps_c", [P, 1], F32)
        g_q = keep("g_q", [P, HD], F32)
        g_k = keep("g_k", [P, HD], F32)
        g_att = keep("g_att", [P, CJ], F32)
        g_conv = keep("g_conv", [P, CJ], F32)
        taps = keep("taps", [P, CJ, 3], F32)
        past_u = keep("past_u", [P, CJ, 2], F32)
        last_u = keep("last_u", [P, CJ, 4], F32)
        b_bc = keep("b_bc", [P, NH], F32)
        x_ss = keep("x_ss", [P, NT], F32)
        x_rms = keep("x_rms", [P, NT], F32)
        x_inv = keep("x_inv", [P, NT], F32)
        qk_ss = keep("qk_ss", [P, 2 * NT, NH], F32)
        qk_rms = keep("qk_rms", [P, 2 * NT, NH], F32)
        qk_inv = keep("qk_inv", [P, 2 * NT, NH], F32)
        wf_raw = keep("wf_raw", [P, KD, NH], F32)
        wf_hi = keep("wf_hi", [P, KD, NH], F32R)
        wf_lo = keep("wf_lo", [P, KD, NH], F32R)
        lf = keep("lf", [P, NB, NH], F32)
        fx = keep("fx", [P, NT, NH], F32)
        f1 = keep("f1", [P, NT, NH], F32)
        f2 = keep("f2", [P, NT, NH], F32)
        f3 = keep("f3", [P, NT, NH], F32)
        f4 = keep("f4", [P, NT, NH], F32)
        total = keep("total", [P, NB, NH], F32)
        before = keep("before", [P, NB, NH], F32)
        neg_c = keep("neg_c", [P, NB, NH], F32)
        neg_c2 = keep("neg_c2", [P, NB, NH, 2], F32R)
        z_rms = keep("z_rms", [P, NT], F32)
        z_inv = keep("z_inv", [P, NT], F32)
        a_ss = keep("a_ss", [P, NT], F32)
        a_rms = keep("a_rms", [P, NT], F32)
        a_inv = keep("a_inv", [P, NT], F32)
        neg_max = keep("neg_max", [P, 2, 1], F32)
        den = keep("den", [P, 2, NT], F32)
        rden = keep("rden", [P, 2, NT], F32)
        qn = keep("qn", [P, NT, AD], F32)
        kn = keep("kn", [P, NT, AD], F32)
        early = at[0]
        silu_a = keep("silu_a", [P, CJ, TOK], F32)
        zg = keep("zg", [P, CJ, TOK], F32)
        stage = at[0]

        def place(first):
            spot = [first]

            def put(name, shape, dt):
                size = 4
                for n in shape[1:]:
                    size *= n
                t = nc.alloc_sbuf_tensor_at(name, shape, dt, offset=spot[0])
                spot[0] += (size + 31) // 32 * 32
                assert spot[0] <= 229368, (name, spot[0])
                return t
            return put, spot

        put, spot = place(early)
        xt = put("xt", [P, 2, DM], F32)
        hn = put("hn", [P, 2, DM], F32)
        g_x = put("g_x", [P, DM], F32)
        sq = put("sq", [P, 2, AD], F32)
        v_out = put("v_out", [P, 2, AD], F32)
        fT = put("fT", [NH, TOK], F32)
        assert spot[0] <= stage
        put, spot = place(stage)
        h_hi = put("h_hi", [P, KD, TOK], F32R)
        h_lo = put("h_lo", [P, KD, TOK], F32R)
        w_hi = put("w_hi", [P, KD * 512], F32R)
        w_lo_at = spot[0]
        w_lo = put("w_lo", [P, KD * 512], F32R)
        w_raw = put("w_raw", [P, KD * 512], F32)
        half = KD * 512 * 2
        put, spot = place(w_lo_at - half)
        u_cv = put("u_cv", [P, TOK + 4], F32)
        assert spot[0] <= w_lo_at
        put, spot = place(w_lo_at + half)
        y_cv = put("y_cv", [P, TOK + 2], F32)
        assert spot[0] <= w_lo_at + 2 * half
        put, spot = place(w_lo_at + 3 * half)
        c_sb = put("c_sb", [P, TOK], F32)
        z_cv = c_sb
        z_sq = put("z_sq", [P, TOK], F32)
        g_cv = put("g_cv", [P, TOK], F32)
        put, spot = place(spot[0])
        z_ss = put("z_ss", [P, TOK], F32)
        x_res, y_part, y_out, mix_f, a_sq = kn[:, 0:2, :], kn[:, 2, :], kn[:, 3:5, :], kn[:, 5:7, :], kn[:, 7, :]
        put, spot = place(stage)
        k_raw = put("k_raw", [P, PB, HD], F32)
        v_raw = put("v_raw", [P, 2, NB, HD], F32)
        k_sp = put("k_sp", [P, NB, 3, HD], F32R)
        q_sp = put("q_sp", [P, NT, 4, HD], F32R)
        kqT = put("kqT", [P, 2, 2 * (NB + NT), P], F32R)
        prob = put("prob", [P, 2, TOK], F32)
        pT = put("pT", [P, 2, 8 * 256], F32)
        o_sum = put("o_sum", [HD, 256], F32)

        ps = ctx.enter_context(nc.psum_tensor("ps", [P, 8, 512], F32))
        ps_r = ps[:, :, :].bitcast(F32R)
        bank_kq = ps[:, 6, :].rearrange("p (b n) -> p b n", n=P)
        all_scores = ps[:, 0:4, :].rearrange("p b n -> p (b n)")

        STEPS = NT * NH
        CHUNKS = 5
        GROUPS = 13
        T_GROUPS = [[list(range(b, min(b + 4, i + 1))) for b in range(0, i + 1, 4)] for i in range(PB)] + [
            [list(range(8)), [8]]]
        T_BEFORE = [sum(len(g) for g in T_GROUPS[:i]) for i in range(NT)]
        T_HEAD = sum(len(g) for g in T_GROUPS)
        assert T_HEAD % 2 == 0 and 4 * GROUPS == 2 * (NB + NT)

        def item_shape(i):
            return (P, (i + 1) * P) if i < PB else (NS, PAST + NS)

        def scores(i):
            return all_scores[:, (i % 2) * 1024:] if i < PB else all_scores

        def t_src(i, g):
            n = T_BEFORE[i] + g
            nb = len(T_GROUPS[i][g])
            if i < PB:
                return ps[:, 4 + n % 2, 0:nb * P].rearrange("p (b q) -> p b q", q=P)
            return ps[:, 4 + n % 2, :] if g == 0 else ps[0:NS, 4 + n % 2, 0:NS]

        def t_dst(i, g):
            t, b = pT[:, (i // 2) % 2, :], T_GROUPS[i][g]
            if i < PB:
                q0 = (i % 2) * P
                return t.rearrange("p (b q) -> p b q", q=256)[:, b[0]:b[-1] + 1, q0:q0 + P]
            return t[:, 0:8 * NS] if g == 0 else t[0:NS, 8 * NS:9 * NS]

        def takes_at(s):
            h, i = divmod(s, NT)
            if i == 0:
                return [(h - 1, 4)] if h else []
            return [(h, i // 2 - 1)] if i % 2 == 0 and s < STEPS else []

        def puts_at(s):
            h, i = divmod(s, NT)
            if i == 0:
                return [(h - 1, 3)] if h else []
            if s >= STEPS:
                return []
            return [(h, i // 2 - 1)] if i % 2 and i > 1 else [(h - 1, 4)] if i == 1 and h else []

        def kq_at(i):
            return [g for g in (2 * i - 2, 2 * i - 1) if 0 <= g < GROUPS]


        sems = {}

        def sem(name):
            if name not in sems:
                sems[name] = ctx.enter_context(nc.semaphore(name))
            return sems[name]

        s_const, s_first, s_wfl, s_ga, s_vpad, s_lastu2 = (sem(n) for n in "s_const s_first s_wfl s_ga s_vpad s_lastu2".split())
        s_x = [sem("s_x0"), sem("s_x1")]
        s_w = [sem(f"s_w{k}") for k in range(KD)]
        s_wf = sem("s_wf")
        s_cast = sem("s_cast")
        s_xsq, s_xrms, s_hn, s_hT, s_hhi, s_hlo = (sem(n) for n in "s_xsq s_xrms s_hn s_hT s_hhi s_hlo".split())
        s_whi, s_wlo, s_wused = sem("s_whi"), sem("s_wlo"), sem("s_wused")
        s_pn, s_ev, s_ss, s_rt, s_norm = (sem(n) for n in "s_pn s_ev s_ss s_rt s_norm".split())
        s_kst, s_vst = [sem("s_kst0"), sem("s_kst1")], [sem("s_vst0"), sem("s_vst1")]
        s_dv = sem("s_dv")
        s_ac = sem("s_ac")

        x_all = [x_prompt[0, i * P:(i + 1) * P, :] for i in range(PB)] + [x_sample[0]]
        k_dst = [k_prompt[0, 0, i * P:(i + 1) * P].rearrange("t h d -> t (h d)") for i in range(PB)] + [
            k_sample[0, 0].rearrange("t h d -> t (h d)")]
        v_dst = [v_prompt[0, 0, i * P:(i + 1) * P].rearrange("t h d -> t (h d)") for i in range(PB)] + [
            v_sample[0, 0].rearrange("t h d -> t (h d)")]
        y_dst = [y_prompt[0, i * P:(i + 1) * P, :] for i in range(PB)] + [y_sample[0]]
        w_rows = w_in[0].rearrange("(k p) n -> p k n", p=P)
        wo_rows = w_out[0].rearrange("(k p) n -> p k n", p=P)

        units = [("a", j, 3 * AD + j * P) for j in range(CJ)]
        for j in range(CJ):
            units += [("C", j, COL_C + j * P), ("h", j, COL_H + j * P), ("B", j, COL_B + j * P), ("g", j, COL_G + j * P)]
        UN = len(units)

        def unit_w(t, u):
            return t[:, (u % 2) * 1024:(u % 2 + 1) * 1024].rearrange("p (k n) -> p k n", k=KD)

        block = ctx.enter_context(nc.Block())

        s_uw = [sem("s_uw0"), sem("s_uw1")]
        s_uhi, s_ulo, s_upe = sem("s_uhi"), sem("s_ulo"), sem("s_upe")
        s_uC, s_uH, s_uB, s_uG, s_uA = (sem(n) for n in "s_uC s_uH s_uB s_uG s_uA".split())
        s_fT, s_fsb, s_fn, s_lf, s_lfst, s_cum, s_negc, s_clf = (sem(n) for n in "s_fT s_fsb s_fn s_lf s_lfst s_cum s_negc s_clf".split())
        s_zv, s_zsq, s_zss, s_zsum, s_zg, s_lastu, s_cst = (sem(n) for n in "s_zv s_zsq s_zss s_zsum s_zg s_lastu s_cst".split())
        s_kr, s_vr = sem("s_kr"), [sem("s_vr0"), sem("s_vr1")]
        s_khi, s_klo, s_ccol = (sem(n) for n in "s_khi s_klo s_ccol".split())
        s_pt, s_evA, s_evV = sem("s_pt"), sem("s_evA"), sem("s_evV")
        s_S, s_max, s_exp, s_T, s_Tcp = (sem(n) for n in "s_S s_max s_exp s_T s_Tcp".split())
        s_O, s_Ocp, s_Ot, s_att, s_rden = (sem(n) for n in "s_O s_Ocp s_Ot s_att s_rden".split())
        s_pad = sem("s_pad")
        s_mT, s_mf, s_mhi, s_mlo = (sem(n) for n in "s_mT s_mf s_mhi s_mlo".split())
        s_zhi, s_zlo = sem("s_zhi"), sem("s_zlo")
        s_wo, s_whi4, s_wlo4, s_wo_used = [sem(f"s_wo{k}") for k in range(KD)], sem("s_whi4"), sem("s_wlo4"), sem("s_wo_used")
        s_xr = [sem("s_xr0"), sem("s_xr1")]
        s_y, s_y1, s_y2, s_yst = sem("s_y"), sem("s_y1"), sem("s_y2"), [sem("s_yst0"), sem("s_yst1")]
        s_asq, s_arms, s_zrms, s_inv = (sem(n) for n in "s_asq s_arms s_zrms s_inv".split())

        WORDER = [4, 5, 6, 7, 0, 1, 2, 3]
        NCONST = 9

        @block.sync
        def _(sp):
            def load_x(i):
                if i >= 2:
                    sp.wait_ge(s_hn, i - 1)
                sp.dma_start(xt[0:rows(i), i % 2, :], x_all[i]).then_inc(s_x[i % 2], 16)

            def load_w(c, k):
                if c:
                    sp.wait_ge(s_wlo, (c - 1) * KD + k + 1)
                sp.dma_start(w_raw[:, k * 512:(k + 1) * 512], w_rows[:, k, c * 512:(c + 1) * 512]).then_inc(s_w[k], 16)

            load_x(0)
            sp.dma_start(g_x[:, :], norm_g[0:1, :].to_broadcast([P, DM])).then_inc(s_first, 16)
            sp.dma_start(ident[:, :], eye).then_inc(s_first, 16)
            load_w(0, 0)
            load_x(1)
            for k in range(1, KD):
                load_w(0, k)
            sp.dma_start(g_q[:, :], q_norm_g[0:1, :].to_broadcast([P, HD])).then_inc(s_const, 16)
            sp.dma_start(g_k[:, :], k_norm_g[0:1, :].to_broadcast([P, HD])).then_inc(s_const, 16)
            sp.dma_start(g_att[:, :], att_out_g).then_inc(s_const, 16)
            sp.dma_start(g_conv[:, :], conv_out_g).then_inc(s_const, 16)
            sp.dma_start(taps[:, :, :], conv_w).then_inc(s_const, 16)
            sp.dma_start(past_u[:, :, :], state_conv).then_inc(s_const, 16)
            sp.dma_start(b_bc[:, :], b_f[0:1, :].to_broadcast([P, NH])).then_inc(s_const, 16)
            sp.dma_start(upto_f[:, :], upto).then_inc(s_const, 16)
            sp.dma_start(ones_f[:, :], future).then_inc(s_const, 16)
            sp.dma_start(wf_raw[:, :, :], w_rows[:, :, COL_F:COL_F + NH]).then_inc(s_wf, 16)
            sp.dma_start(lf[:, NEW + 1:NB, :], cache_logf[0, 0].rearrange("(b p) h -> p b h", p=P)).then_inc(s_clf, 16)
            for i in range(2, NT):
                load_x(i)
            for k in range(KD):
                load_w(1, k)
            for k in range(KD):
                load_w(2, k)
            for i in range(NT):
                sp.wait_ge(s_norm, NT + i + 1)
                sp.dma_start(k_dst[i], kn[0:rows(i), i, :]).then_inc(s_kst[i % 2], 16)
            for u in range(UN):
                if u < 2:
                    sp.wait_ge(s_wlo, 3 * KD)
                else:
                    sp.wait_ge(s_ulo, u - 1)
                sp.dma_start(unit_w(w_raw, u), w_rows[:, :, units[u][2]:units[u][2] + P]).then_inc(s_uw[u % 2], 16)
                if u == 1:
                    for i in range(NT):
                        sp.wait_ge(s_ev, 2 * NT + i + 1)
                        sp.dma_start(v_dst[i], v_out[0:rows(i), i % 2, :]).then_inc(s_vst[i % 2], 16)
            sp.wait_ge(s_lf, 1)
            sp.dma_start(logf_prompt[0, 0].rearrange("(b p) h -> p b h", p=P), lf[:, 0:PB, :]).then_inc(s_lfst, 16)
            sp.dma_start(logf_sample[0, 0], lf[0:NS, NEW, :]).then_inc(s_lfst, 16)
            sp.wait_ge(s_lastu2, 2 * CJ)
            sp.dma_start(conv_last, last_u[:, :, :]).then_inc(s_cst, 16)
            sp.wait_ge(s_vst[0], 16 * 5)
            sp.wait_ge(s_vst[1], 16 * 4)
            for h in range(NH):
                if h == 0:
                    sp.wait_ge(s_upe, 3 * UN)
                else:
                    sp.wait_ge(s_klo, 3 * h)
                sp.dma_start(k_raw[:, :, :], cache_k[0, 0, :, h, :].rearrange("(b p) d -> p b d", p=P)).then_inc(s_kr, 16)
                if h >= 2:
                    sp.wait_ge(s_O, CHUNKS * (h - 1))
                v = v_raw[:, h % 2]
                sp.dma_start(v[:, 0:PB, :], v_prompt[0, 0, :, h, :].rearrange("(b p) d -> p b d", p=P)).then_inc(s_vr[h % 2], 16)
                sp.dma_start(v[0:NS, NEW, :], v_sample[0, 0, :, h, :]).then_inc(s_vr[h % 2], 16)
                sp.dma_start(v[:, NEW + 1:NB, :], cache_v[0, 0, :, h, :].rearrange("(b p) d -> p b d", p=P)).then_inc(s_vr[h % 2], 16)
            def load_wo(n, k):
                b = WORDER[k]
                if n:
                    sp.wait_ge(s_wlo4, k + 1)
                elif k == 0:
                    sp.wait_ge(s_att, CHUNKS * NH)
                sp.dma_start(w_raw[:, k * 512:(k + 1) * 512], wo_rows[:, b, n * 512:(n + 1) * 512]).then_inc(s_wo[k], 16)

            def load_res(e):
                n, i = divmod(e, NT)
                if e >= 2:
                    sp.wait_ge(s_y1, e - 1)
                sp.dma_start(x_res[0:rows(i), e % 2, :], x_all[i][:, n * 512:(n + 1) * 512]).then_inc(s_xr[e % 2], 16)

            def store_y(e):
                n, i = divmod(e, NT)
                sp.wait_ge(s_y2, e + 1)
                sp.dma_start(y_dst[i][:, n * 512:(n + 1) * 512], y_out[0:rows(i), e % 2, :]).then_inc(s_yst[e % 2], 16)

            for k in range(KD):
                load_wo(0, k)
            sp.wait_ge(s_kst[0], 16 * 5)
            sp.wait_ge(s_kst[1], 16 * 4)
            load_res(0)
            load_res(1)
            for k in range(KD):
                load_wo(1, k)
            for e in range(2 * NT):
                if e + 2 < 2 * NT:
                    load_res(e + 2)
                store_y(e)
            sp.wait_ge(s_yst[0], 16 * NT)
            sp.wait_ge(s_yst[1], 16 * NT)
            sp.wait_ge(s_lfst, 32)
            sp.wait_ge(s_cst, 16)

        @block.scalar
        def _(act):
            def square_x(i):
                r = rows(i)
                act.wait_ge(s_x[i % 2], 16 * (i // 2 + 1))
                act.activation(ps[0:r, 4:6, :].rearrange("p b n -> p (b n)"), xt[0:r, i % 2, :], ACT.Square,
                               accum_out=x_ss[0:r, i:i + 1]).then_inc(s_xsq, 1)
                act.wait_ge(s_xsq, i + 1)
                act.activation(x_rms[0:r, i:i + 1], x_ss[0:r, i:i + 1], ACT.Sqrt, scale=1.0 / DM,
                               bias=eps_c[0:r, :]).then_inc(s_xrms, 1)

            def w_high(c, k):
                act.wait_ge(s_w[k], 16 * (c + 1))
                if c:
                    if k < KD - 1:
                        act.wait_ge(s_wused, (c - 1) * (KD - 1) + k + 1)
                    else:
                        act.wait_ge(s_pn, c * NT)
                act.copy(w_hi[:, k * 512:(k + 1) * 512], w_raw[:, k * 512:(k + 1) * 512]).then_inc(s_whi, 1)

            def h_high(i):
                r = rows(i)
                act.wait_ge(s_hT, i + 1)
                act.copy(h_hi[:, :, i * P:i * P + r],
                         ps[:, 2 * (i % 2):2 * (i % 2) + 2, :].rearrange("p b (k t) -> p (b k) t", t=P)[:, :, 0:r]
                         ).then_inc(s_hhi, 1)

            def evict(c, i):
                r, e = rows(i), c * NT + i
                act.wait_ge(s_pn, e + 1)
                src = ps[0:r, 6 + e % 2, :]
                if c == 2:
                    if i >= 2:
                        act.wait_ge(s_vst[i % 2], 16 * (i // 2))
                    act.copy(v_out[0:r, i % 2, :], src).then_inc(s_ev, 1)
                    return
                if e >= 2:
                    act.wait_ge(s_ss, e - 1)
                act.copy((qn if c == 0 else kn)[0:r, i, :], src)
                act.activation(sq[0:r, e % 2, :], src, ACT.Square).then_inc(s_ev, 1)

            def root(e):
                r = rows(e % NT)
                act.wait_ge(s_ss, e + 1)
                act.activation(qk_rms[0:r, e, :], qk_ss[0:r, e, :], ACT.Sqrt, scale=1.0 / HD,
                               bias=eps_c[0:r, :]).then_inc(s_rt, 1)

            act.wait_ge(s_cast, 1)
            square_x(0)
            for k in range(2):
                w_high(0, k)
            h_high(0)
            for k in range(2, KD):
                w_high(0, k)
            for i in range(1, NT):
                square_x(i)
                h_high(i)
                evict(0, i - 1)
                if i >= 2:
                    root(i - 2)
            for k in range(KD):
                w_high(1, k)
            evict(0, NT - 1)
            root(NT - 2)
            for i in range(NT):
                if i == NT - 1:
                    for k in range(KD):
                        w_high(2, k)
                evict(1, i)
                root(NT + i - 1)
            act.wait_ge(s_wf, 16)
            act.copy(wf_hi[:, :, :], wf_raw[:, :, :]).then_inc(s_uhi, 1)
            for i in range(NT):
                evict(2, i)
                if i == 0:
                    root(2 * NT - 1)

            def unit_high(u):
                act.wait_ge(s_uw[u % 2], 16 * (u // 2 + 1))
                act.wait_ge(s_pn, 3 * NT)
                if u >= 2:
                    act.wait_ge(s_upe, 3 * (u - 1))
                act.copy(unit_w(w_hi, u), unit_w(w_raw, u)).then_inc(s_uhi, 1)

            unit_high(0)
            unit_high(1)
            for n, (t0, w) in enumerate(CUTS):
                act.wait_ge(s_fT, n + 1)
                act.copy(fT[:, t0:t0 + w], ps[0:NH, n, 0:w]).then_inc(s_fsb, 1)
            act.wait_ge(s_fn, 2)
            act.activation(f2[:, :, :], f1[:, :, :], ACT.Exp).then_inc(s_fn, 1)
            act.wait_ge(s_fn, 3)
            act.activation(f3[:, :, :], f2[:, :, :], ACT.Ln, bias=1.0).then_inc(s_fn, 1)
            for u, (kind, j, _) in enumerate(units):
                bank = 3 * (u % 2)
                if kind == "C":
                    if j:
                        act.wait_ge(s_zg, j)
                    for n, (t0, w) in enumerate(CUTS):
                        act.wait_ge(s_upe, 3 * u + n + 1)
                        act.copy(c_sb[:, t0:t0 + w], ps[:, bank + n, 0:w]).then_inc(s_uC, 1)
                if kind in "ag":
                    if kind == "g" and j:
                        act.wait_ge(s_zg, j)
                    if kind == "a" and j == 0:
                        act.wait_ge(s_ev, 3 * NT)
                        act.wait_ge(s_vst[0], 16 * 5)
                        act.wait_ge(s_vst[1], 16 * 4)
                        act.wait_ge(s_norm, 2 * NT)
                        act.wait_ge(s_fn, 1)
                    for n, (t0, w) in enumerate(CUTS):
                        act.wait_ge(s_upe, 3 * u + n + 1)
                        dst = silu_a[:, j, t0:t0 + w] if kind == "a" else g_cv[:, t0:t0 + w]
                        act.activation(dst, ps[:, bank + n, 0:w], ACT.Silu).then_inc(s_uA if kind == "a" else s_uG, 1)
                if kind == "B":
                    act.wait_ge(s_zv, 4 * (j + 1))
                    if j:
                        act.wait_ge(s_zss, j)
                    act.activation(z_sq[:, :], z_cv[:, :], ACT.Square).then_inc(s_zsq, 1)
                if u + 2 < UN:
                    unit_high(u + 2)
            act.wait_ge(s_zsum, 1)
            act.activation(z_rms[:, 0:PB], ps[:, 7, 0:2 * PB:2], ACT.Sqrt, scale=1.0 / CD, bias=eps_c[:, :]).then_inc(s_zrms, 1)
            act.activation(z_rms[0:NS, PB:NT], ps[0:NS, 7, 2 * PB:2 * PB + 1], ACT.Sqrt, scale=1.0 / CD,
                           bias=eps_c[0:NS, :]).then_inc(s_zrms, 1)

            def split_high(h):
                if h:
                    act.wait_ge(s_pt, GROUPS * h)
                else:
                    act.wait_ge(s_upe, 3 * UN)
                    act.wait_ge(s_zg, CJ)
                cols = slice(h * HD, (h + 1) * HD)
                act.copy(k_sp[:, 0:NT, 1, :], kn[:, :, cols]).then_inc(s_khi, 1)
                act.copy(q_sp[:, :, 0:2, :], qn[:, :, cols].unsqueeze(2).to_broadcast([P, NT, 2, HD])).then_inc(s_khi, 1)
                act.wait_ge(s_kr, 16 * (h + 1))
                act.copy(k_sp[:, NT:NB, 1, :], k_raw[:, :, :]).then_inc(s_khi, 1)

            def spread(h, g):
                if g % 2 == 0:
                    act.wait_ge(s_pt, GROUPS * h + g + 1)
                    if g == 0 and h >= 2:
                        act.wait_ge(s_S, NT * (h - 1))
                    act.copy(kqT[:, h % 2, 4 * g:4 * g + 4, :], bank_kq).then_inc(s_evA, 1)

            def soft(h, i):
                act.wait_ge(s_max, NT * h + i + 1)
                if h or i >= 2:
                    act.wait_ge(s_T, T_HEAD * h + (T_BEFORE[i - 1] if i >= 2 else 0))
                r, nk = item_shape(i)
                act.activation(prob[0:r, i % 2, 0:nk], scores(i)[0:r, 0:nk], ACT.Exp,
                               bias=neg_max[0:r, i % 2:i % 2 + 1], accum_out=den[0:r, h % 2, i:i + 1]).then_inc(s_exp, 1)

            def o_take(h, c):
                w = 2 * P if c < 4 else NS
                act.wait_ge(s_O, CHUNKS * h + c + 1)
                if h or c:
                    act.wait_ge(s_Ot, CHUNKS * h + c)
                act.copy(o_sum[:, 0:w], ps[0:HD, 7, 0:w]).then_inc(s_Ocp, 1)

            split_high(0)
            for g in range(GROUPS):
                spread(0, g)
            soft(0, 0)
            for s in range(STEPS + 1):
                h, i = divmod(s, NT)
                if s < STEPS and h + 1 < NH:
                    for g in kq_at(i):
                        spread(h + 1, g)
                if s + 1 < STEPS:
                    soft(*divmod(s + 1, NT))
                for c_h, c in takes_at(s):
                    o_take(c_h, c)
                if s < STEPS and i == 0 and h + 1 < NH:
                    split_high(h + 1)

            act.wait_ge(s_att, CHUNKS * NH)

            def z_high(i):
                r = rows(i)
                act.copy(h_hi[:, CJ:KD, i * P:i * P + r], zg[:, :, i * P:i * P + r]).then_inc(s_zhi, 1)

            def wo_high(n, k):
                act.wait_ge(s_wo[k], 16 * (n + 1))
                if n and k < KD - 1:
                    act.wait_ge(s_wo_used, k + 1)
                elif n:
                    act.wait_ge(s_y, NT)
                act.copy(w_hi[:, k * 512:(k + 1) * 512], w_raw[:, k * 512:(k + 1) * 512]).then_inc(s_whi4, 1)

            def mix_high(i):
                r = rows(i)
                act.wait_ge(s_mf, i + 1)
                act.copy(h_hi[:, 0:CJ, i * P:i * P + r],
                         mix_f[:, i % 2, :].rearrange("p (j t) -> p j t", j=CJ)[:, :, 0:r]).then_inc(s_mhi, 1)

            z_high(0)
            for k in range(4):
                wo_high(0, k)
            mix_high(0)
            for k in range(4, KD):
                wo_high(0, k)
            for i in range(NT):
                r = rows(i)
                act.activation(a_sq[0:r, :], qn[0:r, i, :], ACT.Square, accum_out=a_ss[0:r, i:i + 1]).then_inc(s_asq, 1)
                act.wait_ge(s_asq, i + 1)
                act.activation(a_rms[0:r, i:i + 1], a_ss[0:r, i:i + 1], ACT.Sqrt, scale=1.0 / AD, bias=eps_c[0:r, :]).then_inc(s_arms, 1)
                if i == NT - 1:
                    break
                z_high(i + 1)
                mix_high(i + 1)
            for k in range(KD):
                wo_high(1, k)

        @block.gpsimd
        def _(pool):
            for c in range(3):
                for k in range(KD):
                    b = slice(k * 512, (k + 1) * 512)
                    pool.wait_ge(s_whi, c * KD + k + 1)
                    pool.tensor_tensor(w_lo[:, b], w_raw[:, b], w_hi[:, b].bitcast(F32), ALU.subtract).then_inc(s_wlo, 1)
            pool.wait_ge(s_uhi, 1)
            pool.tensor_tensor(wf_lo[:, :, :], wf_raw[:, :, :], wf_hi[:, :, :].bitcast(F32), ALU.subtract).then_inc(s_wfl, 1)
            for u in range(UN):
                pool.wait_ge(s_uhi, u + 2)
                pool.tensor_tensor(unit_w(w_lo, u), unit_w(w_raw, u), unit_w(w_hi, u).bitcast(F32), ALU.subtract).then_inc(s_ulo, 1)
            pool.wait_ge(s_upe, 3 * UN)
            pool.wait_ge(s_zg, CJ)
            pool.memset(k_sp[:, :, 2, :].bitcast(F32), 0.0).then_inc(s_pad, 1)
            pool.memset(q_sp[:, :, 3, 2:HD].bitcast(F32), 0.0).then_inc(s_pad, 1)
            pool.memset(q_sp[:, :, 3, 0:2].bitcast(F32), 1.0).then_inc(s_pad, 1)

            def split_low(h):
                cols = slice(h * HD, (h + 1) * HD)
                pool.wait_ge(s_khi, 3 * h + 1)
                pool.tensor_tensor(k_sp[:, 0:NT, 0, :], kn[:, :, cols], k_sp[:, 0:NT, 1, :].bitcast(F32), ALU.subtract).then_inc(s_klo, 1)
                pool.wait_ge(s_khi, 3 * h + 2)
                pool.tensor_tensor(q_sp[:, :, 2, :], qn[:, :, cols], q_sp[:, :, 0, :].bitcast(F32), ALU.subtract).then_inc(s_klo, 1)
                pool.wait_ge(s_khi, 3 * h + 3)
                pool.tensor_tensor(k_sp[:, NT:NB, 0, :], k_raw[:, :, :], k_sp[:, NT:NB, 1, :].bitcast(F32), ALU.subtract).then_inc(s_klo, 1)

            for h in range(NH):
                split_low(h)
            for n in range(2):
                for k in range(KD):
                    b = slice(k * 512, (k + 1) * 512)
                    pool.wait_ge(s_whi4, n * KD + k + 1)
                    pool.tensor_tensor(w_lo[:, b], w_raw[:, b], w_hi[:, b].bitcast(F32), ALU.subtract).then_inc(s_wlo4, 1)

        @block.vector
        def _(dve):
            done = [0]

            def link(ins):
                done[0] += 1
                ins.then_inc(s_dv, 1)
                dve.wait_ge(s_dv, done[0])

            dve.memset(eps_c[:, :], EPS).then_inc(s_cast, 1)
            dve.memset(qn[NS:P, PB, :], 0.0)
            dve.memset(kn[NS:P, PB, :], 0.0)
            dve.memset(lf[:, NEW, :], 0.0)
            dve.memset(fx[:, :, :], 0.0)

            def normalise(i):
                r = rows(i)
                dve.wait_ge(s_xrms, i + 1)
                link(dve.reciprocal(x_inv[0:r, i:i + 1], x_rms[0:r, i:i + 1]))
                if i >= 2:
                    dve.wait_ge(s_hT, i - 1)
                dve.scalar_tensor_tensor(out=hn[0:r, i % 2, :], in0=xt[0:r, i % 2, :], scalar=x_inv[0:r, i:i + 1],
                                         in1=g_x[0:r, :], op0=ALU.mult, op1=ALU.mult).then_inc(s_hn, 1)

            def h_low(i):
                r = rows(i)
                dve.wait_ge(s_hhi, i + 1)
                cols = slice(i * P, i * P + r)
                dve.tensor_tensor(h_lo[:, :, cols],
                                  ps[:, 2 * (i % 2):2 * (i % 2) + 2, :].rearrange("p b (k t) -> p (b k) t", t=P)[:, :, 0:r],
                                  h_hi[:, :, cols].bitcast(F32), ALU.subtract).then_inc(s_hlo, 1)

            def sums(e):
                r = rows(e % NT)
                dve.wait_ge(s_ev, e + 1)
                dve.tensor_reduce(qk_ss[0:r, e, :], sq[0:r, e % 2, :].rearrange("p (h d) -> p h d", h=NH), AX,
                                  ALU.add).then_inc(s_ss, 1)

            def norm(e):
                c, i = divmod(e, NT)
                r = rows(i)
                t, g = (qn, g_q) if c == 0 else (kn, g_k)
                v = t[0:r, i, :].rearrange("p (h d) -> p h d", h=NH)
                dve.wait_ge(s_rt, e + 1)
                link(dve.reciprocal(qk_inv[0:r, e, :], qk_rms[0:r, e, :]))
                if c == 0:
                    link(dve.tensor_scalar(qk_inv[0:r, e, :], qk_inv[0:r, e, :], HD ** -0.5, None, ALU.mult))
                link(dve.tensor_tensor(v, v, qk_inv[0:r, e, :].unsqueeze(2).to_broadcast([r, NH, HD]), ALU.mult))
                dve.tensor_tensor(v, v, g[0:r, :].unsqueeze(1).to_broadcast([r, NH, HD]), ALU.mult).then_inc(s_norm, 1)

            dve.wait_ge(s_first, 32)
            normalise(0)
            normalise(1)
            h_low(0)
            dve.wait_ge(s_const, 16 * NCONST)
            dve.tensor_copy(ident_r[:, :], ident[:, :]).then_inc(s_cast, 1)
            dve.tensor_copy(ident_b[:, :], ident[:, :]).then_inc(s_cast, 1)
            link(dve.tensor_copy(future_b[:, :], ones_f[:, :]))
            dve.memset(ones_f[:, :], 1.0).then_inc(s_cast, 1)
            for i in range(1, NT):
                if i + 1 < NT:
                    normalise(i + 1)
                h_low(i)
                sums(i - 1)
                if i >= 2:
                    norm(i - 2)
            for e in range(NT - 1, 2 * NT):
                sums(e)
                norm(e - 1)
            norm(2 * NT - 1)

            dve.wait_ge(s_fn, 1)
            dve.tensor_copy(fx[:, 0:PB, :], ps[:, 6, 0:PB * NH].rearrange("p (b h) -> p b h", h=NH)).then_inc(s_dv, 1)
            link(dve.tensor_copy(fx[0:NS, PB, :], ps[0:NS, 6, PB * NH:NT * NH]))
            done[0] += 1
            dve.wait_ge(s_dv, done[0])
            link(dve.tensor_tensor(fx[:, :, :], fx[:, :, :], b_bc[:, :].unsqueeze(1).to_broadcast([P, NT, NH]), ALU.add))
            link(dve.tensor_scalar(f2[:, :, :], fx[:, :, :], -1.0, None, ALU.mult))
            dve.tensor_tensor(f1[:, :, :], fx[:, :, :], f2[:, :, :], ALU.min).then_inc(s_fn, 1)
            dve.wait_ge(s_fn, 4)
            link(dve.tensor_scalar(f4[:, :, :], f2[:, :, :], 1.0, None, ALU.add))
            link(dve.reciprocal(f1[:, :, :], f4[:, :, :]))
            link(dve.tensor_scalar(f4[:, :, :], f4[:, :, :], -1.0, None, ALU.add))
            link(dve.tensor_tensor(f4[:, :, :], f2[:, :, :], f4[:, :, :], ALU.subtract))
            link(dve.tensor_tensor(f4[:, :, :], f4[:, :, :], f1[:, :, :], ALU.mult))
            link(dve.tensor_tensor(f3[:, :, :], f3[:, :, :], f4[:, :, :], ALU.add))
            dve.scalar_tensor_tensor(out=lf[:, 0:NT, :], in0=fx[:, :, :], scalar=0.0, in1=f3[:, :, :], op0=ALU.min,
                                     op1=ALU.subtract).then_inc(s_lf, 1)
            dve.wait_ge(s_cum, 2)
            link(dve.tensor_copy(total[:, :, :], ps[:, 6, NB * NH:2 * NB * NH].rearrange("p (b h) -> p b h", h=NH)))
            dve.memset(before[:, 0, :], 0.0).then_inc(s_dv, 1)
            done[0] += 1
            link(dve.memset(before[:, NEW + 1, :], 0.0))
            for b in range(1, PB):
                dve.tensor_tensor(before[:, b, :], before[:, b - 1, :], total[:, b - 1, :], ALU.add).then_inc(s_dv, 1)
                done[0] += 1
                link(dve.tensor_tensor(before[:, NEW + 1 + b, :], before[:, NEW + b, :], total[:, NEW + b, :], ALU.add))
            link(dve.tensor_tensor(before[:, NEW, :], before[:, NB - 1, :], total[:, NB - 1, :], ALU.add))
            link(dve.scalar_tensor_tensor(out=neg_c[:, :, :], in0=ps[:, 6, 0:NB * NH].rearrange("p (b h) -> p b h", h=NH),
                                          scalar=-1.0, in1=before[:, :, :], op0=ALU.mult, op1=ALU.subtract))
            link(dve.tensor_copy(neg_c2[:, :, :, 0], neg_c[:, :, :]))
            dve.tensor_tensor(neg_c2[:, :, :, 1], neg_c[:, :, :], neg_c2[:, :, :, 0].bitcast(F32), ALU.subtract).then_inc(s_negc, 1)
            for j in range(CJ):
                dve.wait_ge(s_uA, 3 * (j + 1))
                dve.tensor_scalar(silu_a[:, j, :], silu_a[:, j, :], g_att[:, j:j + 1], None, ALU.mult).then_inc(s_ga, 1)
            link(dve.memset(u_cv[:, 0:2], 0.0))
            for u, (kind, j, _) in enumerate(units):
                bank = 3 * (u % 2)
                if kind == "h":
                    if j:
                        dve.wait_ge(s_lastu, j)
                    dve.tensor_copy(u_cv[:, SEQ + 2:SEQ + 4], past_u[:, j, :]).then_inc(s_uH, 1)
                    for n, (t0, w) in enumerate(CUTS):
                        dve.wait_ge(s_upe, 3 * u + n + 1)
                        dve.wait_ge(s_uC, 3 * j + n + 1)
                        if n < 2:
                            dve.tensor_tensor(u_cv[:, 2 + t0:2 + t0 + w], ps[:, bank + n, 0:w], c_sb[:, t0:t0 + w],
                                              ALU.mult).then_inc(s_uH, 1)
                        else:
                            m = SEQ - t0
                            dve.tensor_tensor(u_cv[:, 2 + t0:2 + SEQ], ps[:, bank + n, 0:m], c_sb[:, t0:SEQ], ALU.mult)\
                               .then_inc(s_uH, 1)
                            dve.tensor_tensor(u_cv[:, SEQ + 4:SEQ + 4 + NS], ps[:, bank + n, m:w], c_sb[:, SEQ:TOK],
                                              ALU.mult).then_inc(s_uH, 1)
                    dve.wait_ge(s_uH, 5 * (j + 1))
                    W = TOK + 2
                    dve.tensor_copy(last_u[:, j, 0:2], u_cv[:, SEQ:SEQ + 2]).then_inc(s_lastu2, 1)
                    dve.tensor_copy(last_u[:, j, 2:4], u_cv[:, TOK + 2:TOK + 4]).then_inc(s_lastu2, 1)
                    link(dve.tensor_scalar(y_cv[:, :], u_cv[:, 0:W], taps[:, j, 0:1], None, ALU.mult))
                    link(dve.scalar_tensor_tensor(out=y_cv[:, :], in0=u_cv[:, 1:W + 1], scalar=taps[:, j, 1:2],
                                                  in1=y_cv[:, :], op0=ALU.mult, op1=ALU.add))
                    dve.scalar_tensor_tensor(out=y_cv[:, :], in0=u_cv[:, 2:W + 2], scalar=taps[:, j, 2:3],
                                             in1=y_cv[:, :], op0=ALU.mult, op1=ALU.add).then_inc(s_lastu, 1)
                if kind == "B":
                    dve.wait_ge(s_lastu, j + 1)
                    if j:
                        dve.wait_ge(s_zsq, j)
                        dve.wait_ge(s_zg, j)
                    for n, (t0, w) in enumerate(CUTS):
                        dve.wait_ge(s_upe, 3 * u + n + 1)
                        m = min(w, SEQ - t0)
                        ins = dve.tensor_tensor(z_cv[:, t0:t0 + m], ps[:, bank + n, 0:m], y_cv[:, t0:t0 + m], ALU.mult)
                        if m < w:
                            ins.then_inc(s_zv, 1)
                            ins = dve.tensor_tensor(z_cv[:, SEQ:TOK], ps[:, bank + n, m:w], y_cv[:, SEQ + 2:TOK + 2], ALU.mult)
                        ins.then_inc(s_zv, 1)
                if kind == "g":
                    dve.wait_ge(s_uG, 3 * (j + 1))
                    dve.wait_ge(s_zv, 4 * (j + 1))
                    dve.scalar_tensor_tensor(out=zg[:, j, :], in0=z_cv[:, :], scalar=g_conv[:, j:j + 1], in1=g_cv[:, :],
                                             op0=ALU.mult, op1=ALU.mult).then_inc(s_zg, 1)
                    dve.wait_ge(s_zsq, j + 1)
                    if j == 0:
                        dve.tensor_copy(z_ss[:, :], z_sq[:, :]).then_inc(s_zss, 1)
                    else:
                        dve.wait_ge(s_zss, j)
                        dve.tensor_tensor(z_ss[:, :], z_ss[:, :], z_sq[:, :], ALU.add).then_inc(s_zss, 1)
            dve.wait_ge(s_zrms, 2)
            dve.reciprocal(z_inv[:, 0:PB], z_rms[:, 0:PB]).then_inc(s_inv, 1)
            dve.reciprocal(z_inv[0:NS, PB:NT], z_rms[0:NS, PB:NT]).then_inc(s_inv, 1)

            def c_cols(h):
                if h:
                    dve.wait_ge(s_pt, GROUPS * h)
                else:
                    dve.wait_ge(s_pad, 3)
                    dve.wait_ge(s_negc, 1)
                dve.tensor_copy(k_sp[:, :, 2, 0:2], neg_c2[:, :, h, :].bitcast(F32)).then_inc(s_ccol, 1)

            def spread(h, g):
                if g % 2:
                    dve.wait_ge(s_pt, GROUPS * h + g + 1)
                    if g == 1 and h >= 2:
                        dve.wait_ge(s_S, NT * (h - 1))
                    dve.tensor_copy(kqT[:, h % 2, 4 * g:4 * g + 4, :], bank_kq).then_inc(s_evV, 1)

            def top(h, i):
                dve.wait_ge(s_S, NT * h + i + 1)
                if h or i >= 2:
                    dve.wait_ge(s_exp, NT * h + (i - 1 if i >= 2 else 0))
                r, nk = item_shape(i)
                dve.tensor_reduce(neg_max[0:r, i % 2:i % 2 + 1], scores(i)[0:r, 0:nk], AX, ALU.max, negate=True).then_inc(s_max, 1)

            def t_part(h, i):
                c = i // 2
                for g in range(len(T_GROUPS[i])):
                    dve.wait_ge(s_T, T_HEAD * h + T_BEFORE[i] + g + 1)
                    if i % 2 == 0 and g == 0 and c >= 2:
                        dve.wait_ge(s_O, CHUNKS * h + c - 1)
                    elif i == 0 and g == 0 and h:
                        dve.wait_ge(s_O, CHUNKS * h)
                    dve.tensor_copy(t_dst(i, g), t_src(i, g)).then_inc(s_Tcp, 1)

            def o_put(h, c):
                i0, i1 = (2 * c, 2 * c + 2) if c < 4 else (PB, NT)
                m, n = rows(i0), i1 - i0
                r = rden[0:m, h % 2, i0:i1]
                dve.wait_ge(s_exp, NT * h + i1)
                dve.reciprocal(r, den[0:m, h % 2, i0:i1]).then_inc(s_rden, 1)
                dve.wait_ge(s_rden, CHUNKS * h + c + 1)
                dve.wait_ge(s_Ot, CHUNKS * h + c + 1)
                dve.tensor_tensor(qn[0:m, i0:i1, h * HD:(h + 1) * HD],
                                  ps[0:m, 7, 256:256 + n * HD].rearrange("p (i d) -> p i d", i=n),
                                  r.unsqueeze(2).to_broadcast([m, n, HD]), ALU.mult).then_inc(s_att, 1)

            c_cols(0)
            for g in range(GROUPS):
                spread(0, g)
            top(0, 0)
            for s in range(STEPS + 1):
                h, i = divmod(s, NT)
                for g in kq_at(i - 1) if s < STEPS and h + 1 < NH and i else ():
                    spread(h + 1, g)
                if s + 1 < STEPS:
                    top(*divmod(s + 1, NT))
                for c_h, c in puts_at(s):
                    o_put(c_h, c)
                if s < STEPS:
                    t_part(h, i)
                if s < STEPS and i == 0 and h + 1 < NH:
                    c_cols(h + 1)
            o_put(NH - 1, 4)

            def z_low(i):
                cols = slice(i * P, i * P + rows(i))
                dve.wait_ge(s_zhi, i + 1)
                dve.tensor_tensor(h_lo[:, CJ:KD, cols], zg[:, :, cols], h_hi[:, CJ:KD, cols].bitcast(F32), ALU.subtract).then_inc(s_zlo, 1)

            def mix(i):
                r = rows(i)
                cols = slice(i * P, i * P + r)
                m = mix_f[:, i % 2, :].rearrange("p (j t) -> p j t", j=CJ)[:, :, 0:r]
                dve.wait_ge(s_mT, i + 1)
                dve.tensor_tensor(m, ps[:, i % 2, :].rearrange("p (j t) -> p j t", j=CJ)[:, :, 0:r], silu_a[:, :, cols],
                                  ALU.mult).then_inc(s_mf, 1)

            def mix_low(i):
                r = rows(i)
                cols = slice(i * P, i * P + r)
                m = mix_f[:, i % 2, :].rearrange("p (j t) -> p j t", j=CJ)[:, :, 0:r]
                dve.wait_ge(s_mhi, i + 1)
                dve.tensor_tensor(h_lo[:, 0:CJ, cols], m, h_hi[:, 0:CJ, cols].bitcast(F32), ALU.subtract).then_inc(s_mlo, 1)

            def result(e):
                n, i = divmod(e, NT)
                r = rows(i)
                bank = 2 + 2 * (e % 3)
                if n == 0:
                    dve.wait_ge(s_arms, i + 1)
                    dve.reciprocal(a_inv[0:r, i:i + 1], a_rms[0:r, i:i + 1]).then_inc(s_inv, 1)
                    dve.wait_ge(s_inv, 3 + i)
                dve.wait_ge(s_y, e + 1)
                dve.wait_ge(s_xr[e % 2], 16 * (e // 2 + 1))
                if e:
                    dve.wait_ge(s_y2, e)
                dve.scalar_tensor_tensor(out=y_part[0:r, :], in0=ps[0:r, bank, :], scalar=z_inv[0:r, i:i + 1],
                                         in1=x_res[0:r, e % 2, :], op0=ALU.mult, op1=ALU.add).then_inc(s_y1, 1)
                dve.wait_ge(s_y1, e + 1)
                if e >= 2:
                    dve.wait_ge(s_yst[e % 2], 16 * (e // 2))
                dve.scalar_tensor_tensor(out=y_out[0:r, e % 2, :], in0=ps[0:r, bank + 1, :], scalar=a_inv[0:r, i:i + 1],
                                         in1=y_part[0:r, :], op0=ALU.mult, op1=ALU.add).then_inc(s_y2, 1)

            z_low(0)
            mix(0)
            mix_low(0)
            for i in range(1, NT):
                z_low(i)
                mix(i)
                mix_low(i)
                result(i - 1)
            for e in range(NT - 1, 2 * NT):
                result(e)

        @block.tensor
        def _(pe):
            def three(out, a_hi, a_lo, b_hi, b_lo, first, last):
                pe.matmul(out, a_hi, b_hi, start=first, stop=False)
                pe.matmul(out, a_hi, b_lo, start=False, stop=False)
                return pe.matmul(out, a_lo, b_hi, start=False, stop=last)

            def turn_x(i):
                r = rows(i)
                pe.wait_ge(s_hn, i + 1)
                if i >= 2:
                    pe.wait_ge(s_hlo, i - 1)
                for k in range(KD):
                    t = pe.transpose(ps[:, 2 * (i % 2) + k // 4, (k % 4) * P:(k % 4) * P + r],
                                     hn[0:r, i % 2, k * P:(k + 1) * P], ident[0:r, 0:r])
                t.then_inc(s_hT, 1)

            def project(c, i):
                e, r = c * NT + i, rows(i)
                if e >= 2:
                    pe.wait_ge(s_ev, e - 1)
                if c == 0:
                    pe.wait_ge(s_hlo, i + 1)
                cols = slice(i * P, i * P + r)
                for k in range(KD):
                    if i == 0:
                        pe.wait_ge(s_wlo, c * KD + k + 1)
                    w = slice(k * 512, (k + 1) * 512)
                    m = three(ps[0:r, 6 + e % 2, :], h_hi[:, k, cols], h_lo[:, k, cols], w_hi[:, w], w_lo[:, w], k == 0, k == KD - 1)
                    if i == NT - 1 and k < KD - 1:
                        m.then_inc(s_wused, 1)
                m.then_inc(s_pn, 1)

            pe.wait_ge(s_first, 32)
            turn_x(0)
            turn_x(1)
            for c in range(3):
                for i in range(NT):
                    if c == 0 and i + 1 < NT and i:
                        turn_x(i + 1)
                    project(c, i)
            pe.wait_ge(s_wfl, 1)
            for n, (t0, w) in enumerate(CUTS):
                if n == 0:
                    pe.wait_ge(s_hlo, NT)
                for k in range(KD):
                    m = three(ps[0:NH, n, 0:w], wf_hi[:, k, :], wf_lo[:, k, :], h_hi[:, k, t0:t0 + w], h_lo[:, k, t0:t0 + w],
                              k == 0, k == KD - 1)
                m.then_inc(s_fT, 1)
            pe.wait_ge(s_fsb, 3)
            pe.wait_ge(s_ev, 3 * NT)
            for i in range(NT):
                t = pe.transpose(ps[0:rows(i), 6, i * NH:(i + 1) * NH], fT[:, i * P:i * P + rows(i)], ident[0:NH, 0:NH])
            t.then_inc(s_fn, 1)

            def cumulate():
                pe.wait_ge(s_lf, 1)
                pe.wait_ge(s_clf, 16)
                pe.matmul(ps[:, 6, 0:NB * NH], upto_f[:, :], lf[:, :, :], start=True, stop=True).then_inc(s_cum, 1)
                pe.matmul(ps[:, 6, NB * NH:2 * NB * NH], ones_f[:, :], lf[:, :, :], start=True, stop=True).then_inc(s_cum, 1)

            for u, (kind, j, _) in enumerate(units):
                bank = 3 * (u % 2)
                if u == 0:
                    pe.wait_ge(s_fsb, 3)
                if u >= 2:
                    k2, j2, _ = units[u - 2]
                    if k2 == "a":
                        pe.wait_ge(s_uA, 3 * (j2 + 1))
                    elif k2 == "C":
                        pe.wait_ge(s_uC, 3 * (j2 + 1))
                    elif k2 == "h":
                        pe.wait_ge(s_uH, 5 * (j2 + 1))
                    elif k2 == "B":
                        pe.wait_ge(s_zv, 4 * (j2 + 1))
                    else:
                        pe.wait_ge(s_uG, 3 * (j2 + 1))
                pe.wait_ge(s_ulo, u + 1)
                wh, wl = unit_w(w_hi, u), unit_w(w_lo, u)
                for n, (t0, w) in enumerate(CUTS):
                    for k in range(KD):
                        m = three(ps[:, bank + n, 0:w], wh[:, k, :], wl[:, k, :], h_hi[:, k, t0:t0 + w], h_lo[:, k, t0:t0 + w],
                                  k == 0, k == KD - 1)
                    m.then_inc(s_upe, 1)
                if u == 1:
                    cumulate()
            pe.wait_ge(s_zss, CJ)
            for i in range(NT):
                r = rows(i)
                m = pe.matmul(ps[0:r, 7, 2 * i:2 * i + 2], z_ss[:, i * P:i * P + r], ones_f[:, 0:2], start=True, stop=True)
            m.then_inc(s_zsum, 1)

            def kq_group(h, g):
                if g == 0:
                    pe.wait_ge(s_klo, 3 * (h + 1))
                    pe.wait_ge(s_ccol, h + 1)
                    if h:
                        pe.wait_ge(s_evA, 7 * h)
                elif g % 2:
                    pe.wait_ge(s_evA, 7 * h + (g + 1) // 2)
                else:
                    pe.wait_ge(s_evV, 6 * h + g // 2)
                for n in range(4):
                    b, part = divmod(4 * g + n, 2)
                    if b < NB:
                        src = k_sp[:, b, part:part + 2, :]
                    else:
                        src = q_sp[:, b - NB, 2 * part:2 * part + 2, :]
                    t = pe.transpose(ps_r[:, 6, n * P:(n + 1) * P], src.rearrange("p s d -> p (s d)"), ident_r[:, :])
                t.then_inc(s_pt, 1)

            def score(h, i):
                if i == 0:
                    pe.wait_ge(s_evA, 7 * (h + 1))
                    pe.wait_ge(s_evV, 6 * (h + 1))
                if h and i < 2:
                    pe.wait_ge(s_exp, NT * h)
                elif i >= 2:
                    pe.wait_ge(s_exp, NT * h + (i if i == 8 else i - 1))
                m = rows(i)
                out = scores(i)
                if i < PB:
                    pieces = [(b, min(b + 4, i + 1), b * P) for b in range(0, i + 1, 4)]
                else:
                    pieces = [(NT, NT + 4, 0), (NT + 4, NB, 512), (NEW, NEW + 1, PAST)]
                par = kqT[:, h % 2].rearrange("p (b s) n -> p b s n", s=2)
                for b0, b1, col in pieces:
                    width = P if b0 != NEW or i < PB else NS
                    own = b1 == i + 1 if i < PB else b0 == NEW
                    n = (b1 - b0) * width
                    for part in range(2):
                        ins = pe.matmul(out[0:m, col:col + n], par[:, NB + i, part, 0:m], par[:, b0:b1, part, 0:width],
                                        start=part == 0, stop=part == 1 and not own)
                    if own:
                        ins = pe.matmul(out[0:m, col + n - width:col + n], ident_b[0:m, 0:m], future_b[0:m, 0:width],
                                        start=False, stop=True)
                ins.then_inc(s_S, 1)

            def turn_p(h, i):
                pe.wait_ge(s_exp, NT * h + i + 1)
                m = rows(i)
                for g, blocks in enumerate(T_GROUPS[i]):
                    n = T_BEFORE[i] + g
                    if h or n >= 2:
                        pe.wait_ge(s_Tcp, T_HEAD * h + n - 1)
                    for b in blocks:
                        w = P if b < 8 else NS
                        t = pe.transpose(ps[0:w, 4 + n % 2, (b - blocks[0]) * m:(b - blocks[0] + 1) * m],
                                         prob[0:m, i % 2, b * P:b * P + w], ident[0:m, 0:m])
                    t.then_inc(s_T, 1)

            def weigh(h, c):
                if c == 0:
                    pe.wait_ge(s_vr[h % 2], 48 * (h // 2 + 1))
                if h or c:
                    pe.wait_ge(s_att, CHUNKS * h + c)
                pe.wait_ge(s_Tcp, T_HEAD * h + (T_BEFORE[2 * c + 2] if c < 4 else T_HEAD))
                t, v = pT[:, c % 2, :], v_raw[:, h % 2]
                if c < 4:
                    for b in range(2 * c + 2):
                        q0 = 0 if b <= 2 * c else P
                        ins = pe.matmul(ps[0:HD, 7, q0:256], v[:, b, :], t[:, b * 256 + q0:(b + 1) * 256], start=b == 0,
                                        stop=b == 2 * c + 1, skip_group_check=True)
                else:
                    for n in range(9):
                        k = P if n < 8 else NS
                        b = NT + n if n < 8 else NEW
                        ins = pe.matmul(ps[0:HD, 7, 0:NS], v[0:k, b, :], t[0:k, n * NS:(n + 1) * NS], start=n == 0,
                                        stop=n == 8, skip_group_check=True)
                ins.then_inc(s_O, 1)

            def o_turn(h, c):
                pe.wait_ge(s_Ocp, CHUNKS * h + c + 1)
                if h or c:
                    pe.wait_ge(s_att, CHUNKS * h + c)
                for n in range(2 if c < 4 else 1):
                    m = P if c < 4 else NS
                    t = pe.transpose(ps[0:m, 7, 256 + n * HD:256 + (n + 1) * HD], o_sum[:, n * P:n * P + m], ident[0:HD, 0:HD])
                t.then_inc(s_Ot, 1)

            for g in range(GROUPS):
                kq_group(0, g)
            score(0, 0)
            for s in range(STEPS + 1):
                h, i = divmod(s, NT)
                ahead = kq_at(i) if s < STEPS and h + 1 < NH else []
                if s + 1 < STEPS:
                    score(*divmod(s + 1, NT))
                for g in ahead[0:1]:
                    kq_group(h + 1, g)
                for c_h, c in puts_at(s):
                    o_turn(c_h, c)
                if s < STEPS:
                    turn_p(h, i)
                for c_h, c in takes_at(s):
                    weigh(c_h, c)
                for g in ahead[1:]:
                    kq_group(h + 1, g)
            o_turn(NH - 1, 4)

            def turn_mix(i):
                r = rows(i)
                if i == 0:
                    pe.wait_ge(s_att, CHUNKS * NH)
                if i >= 2:
                    pe.wait_ge(s_mf, i - 1)
                for j in range(CJ):
                    t = pe.transpose(ps[:, i % 2, j * P:j * P + r], qn[0:r, i, j * P:(j + 1) * P], ident[0:r, 0:r])
                t.then_inc(s_mT, 1)

            turn_mix(0)
            for e in range(2 * NT):
                n, i = divmod(e, NT)
                r = rows(i)
                bank = 2 + 2 * (e % 3)
                cols = slice(i * P, i * P + r)
                if n == 0 and i + 1 < NT:
                    turn_mix(i + 1)
                if e >= 3:
                    pe.wait_ge(s_y2, e - 2)
                for k in range(KD):
                    if i == 0:
                        pe.wait_ge(s_wlo4, n * KD + k + 1)
                    if n == 0 and k == 0:
                        pe.wait_ge(s_zlo, i + 1)
                    if n == 0 and k == 4:
                        pe.wait_ge(s_mlo, i + 1)
                    w = slice(k * 512, (k + 1) * 512)
                    m = three(ps[0:r, bank + k // 4, :], h_hi[:, WORDER[k], cols], h_lo[:, WORDER[k], cols], w_hi[:, w], w_lo[:, w],
                              k % 4 == 0, k % 4 == 3)
                    if n == 0 and i == NT - 1 and k < KD - 1:
                        m.then_inc(s_wo_used, 1)
                    if k == KD - 1:
                        m.then_inc(s_y, 1)
    return nc


_OUTS = [("y_prompt", (1, SEQ, DM)), ("y_sample", (1, NS, DM)), ("k_prompt", (1, 1, SEQ, NH, HD)),
         ("v_prompt", (1, 1, SEQ, NH, HD)), ("logf_prompt", (1, 1, SEQ, NH)), ("k_sample", (1, 1, NS, NH, HD)),
         ("v_sample", (1, 1, NS, NH, HD)), ("logf_sample", (1, 1, NS, NH)), ("conv_last", (P, CJ, 4))]


def kernel(**inputs):
    import numpy as np
    import concourse.bacc as bacc
    from concourse.bass_utils import run_bass_kernel_spmd

    def by_channel(a):
        return np.ascontiguousarray(a.reshape(-1, CJ, P).transpose(2, 1, 0))

    a = {n: np.asarray(v) for n, v in inputs.items()}
    for n in ("state_conv", "conv_w"):
        a[n] = by_channel(a[n].reshape(-1, CD))
    for n in ("att_out_g", "conv_out_g"):
        a[n] = by_channel(a[n])[:, :, 0]
    q = np.arange(P)
    a["eye"] = np.eye(P, dtype=np.float32)
    a["future"] = np.where(q[None, :] > q[:, None], np.float32(-1e30), np.float32(0))
    a["upto"] = (q[:, None] <= q[None, :]).astype(np.float32)
    nc = bacc.Bacc("TRN2", target_bir_lowering=False, num_devices=1)
    arrays, args = {}, {}
    for n, v in a.items():
        v = np.ascontiguousarray(v)
        arrays[f"in_{n}"] = v
        args[n] = nc.dram_tensor(f"in_{n}", v.shape, F32, kind="ExternalInput").ap()
    for n, shape in _OUTS:
        args[n] = nc.dram_tensor(f"out_{n}", shape, F32, kind="ExternalOutput").ap()
    build(nc, **args)
    r = run_bass_kernel_spmd(nc, [arrays], core_ids=[0]).results[0]
    last = np.asarray(r["out_conv_last"]).transpose(2, 1, 0).reshape(4, CD)
    return (r["out_y_prompt"], r["out_y_sample"], r["out_k_prompt"], r["out_v_prompt"], r["out_logf_prompt"],
            last[0:2].reshape(1, 1, 2, CD), r["out_k_sample"], r["out_v_sample"], r["out_logf_sample"],
            last[2:4].reshape(1, 1, 2, CD))
```

```python
from contextlib import ExitStack

import concourse.bass as bass
from concourse import mybir

ALU = mybir.AluOpType
ACT = mybir.ActivationFunctionType
AX = mybir.AxisListType.X
F32 = mybir.dt.float32
F32R = mybir.dt.float32r
BF16 = mybir.dt.bfloat16

P = 128
DM = 1024
KD = DM // P
NH = 8
HD = 64
AD = NH * HD
CD = 512
CJ = CD // P
SEQ = 1024
NS = 64
PAST = 1024
TOK = SEQ + NS
NT = 9
PB = SEQ // P
NB = 2 * PB + 1
NEW = PB
EPS = 1e-6
CUTS = [(0, 384), (384, 384), (768, 320)]
COL_F = 4 * AD
COL_B, COL_C, COL_H, COL_G = (COL_F + NH + i * CD for i in range(4))


def rows(i):
    return P if i < PB else NS


def build(nc, x_prompt, x_sample, cache_k, cache_v, cache_logf, state_conv, norm_g, w_in, b_f,
          q_norm_g, k_norm_g, conv_w, att_out_g, conv_out_g, w_out, eye, future, upto,
          y_prompt, y_sample, k_prompt, v_prompt, logf_prompt, k_sample, v_sample, logf_sample,
          conv_last):
    ctx = ExitStack()
    with ctx:
        at = [16512]

        def keep(name, shape, dt):
            size = 2 if dt == BF16 else 4
            for n in shape[1:]:
                size *= n
            t = nc.alloc_sbuf_tensor_at(name, shape, dt, offset=at[0])
            at[0] += (size + 31) // 32 * 32
            return t

        ident = keep("ident", [P, P], F32)
        ident_r = keep("ident_r", [P, P], F32R)
        ident_b = keep("ident_b", [P, P], BF16)
        future_b = keep("future_b", [P, P], BF16)
        upto_f = keep("upto_f", [P, P], F32)
        ones_f = keep("ones_f", [P, P], F32)
        eps_c = keep("eps_c", [P, 1], F32)
        g_q = keep("g_q", [P, HD], F32)
        g_k = keep("g_k", [P, HD], F32)
        g_att = keep("g_att", [P, CJ], F32)
        g_conv = keep("g_conv", [P, CJ], F32)
        taps = keep("taps", [P, CJ, 3], F32)
        past_u = keep("past_u", [P, CJ, 2], F32)
        last_u = keep("last_u", [P, CJ, 4], F32)
        b_bc = keep("b_bc", [P, NH], F32)
        x_ss = keep("x_ss", [P, NT], F32)
        x_rms = keep("x_rms", [P, NT], F32)
        x_inv = keep("x_inv", [P, NT], F32)
        qk_ss = keep("qk_ss", [P, 2 * NT, NH], F32)
        qk_rms = keep("qk_rms", [P, 2 * NT, NH], F32)
        qk_inv = keep("qk_inv", [P, 2 * NT, NH], F32)
        wf_raw = keep("wf_raw", [P, KD, NH], F32)
        wf_sp = keep("wf_sp", [P, KD, 2 * NH], F32R)
        lf = keep("lf", [P, NB, NH], F32)
        fx = keep("fx", [P, NT, NH], F32)
        f1 = keep("f1", [P, NT, NH], F32)
        f2 = keep("f2", [P, NT, NH], F32)
        f3 = keep("f3", [P, NT, NH], F32)
        f4 = keep("f4", [P, NT, NH], F32)
        total = keep("total", [P, NB, NH], F32)
        before = keep("before", [P, NB, NH], F32)
        neg_c = keep("neg_c", [P, NB, NH], F32)
        neg_c2 = keep("neg_c2", [P, NB, NH, 2], F32R)
        warm = keep("warm", [P, 1], F32)
        z_rms = keep("z_rms", [P, NT], F32)
        z_inv = keep("z_inv", [P, NT], F32)
        a_ss = keep("a_ss", [P, NT], F32)
        a_rms = keep("a_rms", [P, NT], F32)
        a_inv = keep("a_inv", [P, NT], F32)
        neg_max = keep("neg_max", [P, 2, 1], F32)
        den = keep("den", [P, 2, NT], F32)
        rden = keep("rden", [P, 2, NT], F32)
        qn = keep("qn", [P, NT, AD], F32)
        kn = keep("kn", [P, NT, AD], F32)
        early = at[0]
        silu_a = keep("silu_a", [P, CJ, TOK], F32)
        zg = keep("zg", [P, CJ, TOK], F32)
        stage = at[0]

        def place(first):
            spot = [first]

            def put(name, shape, dt):
                size = 4
                for n in shape[1:]:
                    size *= n
                t = nc.alloc_sbuf_tensor_at(name, shape, dt, offset=spot[0])
                spot[0] += (size + 31) // 32 * 32
                assert spot[0] <= 229368, (name, spot[0])
                return t
            return put, spot

        put, spot = place(early)
        xt = put("xt", [P, 2, DM], F32)
        hn = put("hn", [P, 2, DM], F32)
        g_x = put("g_x", [P, DM], F32)
        sq = put("sq", [P, 2, AD], F32)
        v_out = put("v_out", [P, 2, AD], F32)
        fT = put("fT", [2 * NH, TOK], F32)
        assert spot[0] <= stage
        put, spot = place(stage)
        h_hi = put("h_hi", [P, KD, TOK], F32R)
        h_lo = put("h_lo", [P, KD, TOK], F32R)
        w_hi = put("w_hi", [P, KD * 512], F32R)
        w_lo_at = spot[0]
        w_lo = put("w_lo", [P, KD * 512], F32R)
        w_raw = put("w_raw", [P, KD * 512], F32)
        h_s = put("h_s", [P, KD, 2, NS], F32R)
        s_part = put("s_part", [NS, 512], F32)
        s_whole = put("s_whole", [NS, 512], F32)
        half = KD * 512 * 2
        put, spot = place(w_lo_at - half)
        u_cv = put("u_cv", [P, TOK + 4], F32)
        u_cv_end = spot[0]
        assert spot[0] <= w_lo_at
        put, spot = place(w_lo_at + half)
        y_cv = put("y_cv", [P, TOK + 2], F32)
        assert spot[0] <= w_lo_at + 2 * half
        put, spot = place(w_lo_at + 3 * half)
        c_sb = put("c_sb", [P, TOK], F32)
        z_cv = c_sb
        z_sq = put("z_sq", [P, TOK], F32)
        g_cv = put("g_cv", [P, TOK], F32)
        z_ss_at = spot[0]
        z_ss = put("z_ss", [P, TOK], F32)
        x_res, y_part, y_out, mix_f, a_sq = kn[:, 0:2, :], kn[:, 2, :], kn[:, 3:5, :], kn[:, 5:7, :], kn[:, 7, :]
        put, spot = place(stage)
        kqT = put("kqT", [P, 2, 2 * (NB + NT), P], F32R)
        k_sp_at = spot[0]
        k_sp = put("k_sp", [P, NB, 3, HD], F32R)
        q_sp = put("q_sp", [P, NT, 4, HD], F32R)
        assert spot[0] <= u_cv_end
        put, spot = place(u_cv_end)
        k_raw = put("k_raw", [P, PB, HD], F32)
        assert spot[0] <= w_lo_at
        put, spot = place(stage)
        w4_raw = put("w4_raw", [P, KD * 512], F32)
        m_hi = put("m_hi", [P, KD, TOK], F32R)
        assert spot[0] <= k_sp_at
        put, spot = place(k_sp_at)
        w4_hi = put("w4_hi", [P, KD * 512], F32R)
        w4_lo = put("w4_lo", [P, KD * 512], F32R)
        w4_end = spot[0]
        m_lo = put("m_lo", [P, KD, TOK], F32R)
        assert spot[0] <= z_ss_at
        put, spot = place(w4_end)
        prob = put("prob", [P, 2, TOK], F32)
        pT = put("pT", [P, 2, 8 * 256], F32)
        v_raw = put("v_raw", [P, 2, NB, HD], F32)
        o_sum = put("o_sum", [HD, 256], F32)
        assert spot[0] <= z_ss_at

        ps = ctx.enter_context(nc.psum_tensor("ps", [P, 8, 512], F32))
        ps_r = ps[:, :, :].bitcast(F32R)
        KQ_FIRST = (6, 0, 1, 2, 3, 4, 5)

        def kq_bank(h, g):
            return 6 if h else KQ_FIRST[g % len(KQ_FIRST)]

        def bank_kq(h, g):
            return ps[:, kq_bank(h, g), :].rearrange("p (b n) -> p b n", n=P)

        all_scores = ps[:, 0:4, :].rearrange("p b n -> p (b n)")

        STEPS = NT * NH
        CHUNKS = 5
        GROUPS = 13
        T_GROUPS = [[list(range(b, min(b + 4, i + 1))) for b in range(0, i + 1, 4)] for i in range(PB)] + [
            [list(range(8)), [8]]]
        T_BEFORE = [sum(len(g) for g in T_GROUPS[:i]) for i in range(NT)]
        T_HEAD = sum(len(g) for g in T_GROUPS)
        T_LIST = [(i, g) for i in range(NT) for g in range(len(T_GROUPS[i]))]
        T_SECOND = [i for i in range(NT) if len(T_GROUPS[i]) > 1]
        assert T_HEAD % 2 == 0 and 4 * GROUPS == 2 * (NB + NT)

        def item_shape(i):
            return (P, (i + 1) * P) if i < PB else (NS, PAST + NS)

        def scores(i):
            return all_scores[:, (i % 2) * 1024:] if i < PB else all_scores[:, 512:]

        def t_src(i, g):
            n = T_BEFORE[i] + g
            nb = len(T_GROUPS[i][g])
            if i < PB:
                return ps[:, 4 + n % 2, 0:nb * P].rearrange("p (b q) -> p b q", q=P)
            return ps[:, 4 + n % 2, :] if g == 0 else ps[0:NS, 4 + n % 2, 0:NS]

        def t_dst(i, g):
            t, b = pT[:, (i // 2) % 2, :], T_GROUPS[i][g]
            if i < PB:
                q0 = (i % 2) * P
                return t.rearrange("p (b q) -> p b q", q=256)[:, b[0]:b[-1] + 1, q0:q0 + P]
            return t[:, 0:8 * NS] if g == 0 else t[0:NS, 8 * NS:9 * NS]

        def p_read(h, i, g):
            if g == 0:
                return p_taken_dve, NT * h + i + 1
            return p_taken_act, len(T_SECOND) * h + T_SECOND.index(i) + 1

        def takes_at(s):
            h, i = divmod(s, NT)
            if i == 0:
                return [(h - 1, 4)] if h else []
            return [(h, i // 2 - 1)] if i % 2 == 0 and s < STEPS else []

        def puts_at(s):
            h, i = divmod(s, NT)
            if i == 0:
                return [(h - 1, 3)] if h else []
            if s >= STEPS:
                return []
            return [(h, i // 2 - 1)] if i % 2 and i > 1 else [(h - 1, 4)] if i == 1 and h else []

        def kq_at(i):
            return KQ_STEPS[i]

        KQ_STEPS = [[0, 1], [2], [3, 4], [5], [6, 7], [8, 9], [10, 11], [12], []]
        KQ_DVE = [0] + [groups[1] for groups in KQ_STEPS[1:] if len(groups) > 1]
        KQ_LATE = (0, 5)

        def by_dve(h, g):
            return g in KQ_DVE if h else g % 2 == 1

        def kq_read(h, g):
            before = [(h2, g2) for h2 in range(h + 1) for g2 in range(GROUPS if h2 < h else g + 1)]
            mine = by_dve(h, g)
            return (kq_taken_dve if mine else kq_taken_act), sum(by_dve(*b) == mine for b in before)

        sems = {}

        def sem(name):
            if name not in sems:
                sems[name] = ctx.enter_context(nc.semaphore(name))
            return sems[name]

        first_loaded = sem("first_loaded")
        small_loaded = sem("small_loaded")
        x_loaded = [sem("x_loaded_0"), sem("x_loaded_1")]
        w_loaded = [sem(f"w_loaded_{k}") for k in range(KD)]
        wf_loaded = sem("wf_loaded")
        unit_loaded = [sem("unit_loaded_0"), sem("unit_loaded_1")]
        cached_lf_loaded = sem("cached_lf_loaded")
        cached_k_loaded = sem("cached_k_loaded")
        v_loaded = [sem("v_loaded_0"), sem("v_loaded_1")]
        wo_loaded = [sem(f"wo_loaded_{k}") for k in range(KD)]
        residual_loaded = [sem("residual_loaded_0"), sem("residual_loaded_1")]
        k_stored = [sem("k_stored_0"), sem("k_stored_1")]
        v_stored = [sem("v_stored_0"), sem("v_stored_1")]
        lf_stored = sem("lf_stored")
        conv_stored = sem("conv_stored")
        y_stored = [sem("y_stored_0"), sem("y_stored_1")]
        consts_made = sem("consts_made")
        x_squared = sem("x_squared")
        x_rms_made = sem("x_rms_made")
        h_normed = sem("h_normed")
        h_turned = sem("h_turned")
        h_high_made = sem("h_high_made")
        h_low_made = sem("h_low_made")
        w_high_made = sem("w_high_made")
        w_low_made_pool = sem("w_low_made_pool")
        w_low_made_dve = sem("w_low_made_dve")
        w_block_used = sem("w_block_used")
        projected = sem("projected")
        proj_taken = sem("proj_taken")
        heads_summed = sem("heads_summed")
        heads_rooted = sem("heads_rooted")
        heads_normed = sem("heads_normed")
        dve_chain = sem("dve_chain")
        sample_split = sem("sample_split")
        halves_taken = sem("halves_taken")
        whole_made = sem("whole_made")
        wf_split = sem("wf_split")
        f_logits_made = sem("f_logits_made")
        f_logits_taken = sem("f_logits_taken")
        f_step = sem("f_step")
        lf_made = sem("lf_made")
        sums_made = sem("sums_made")
        neg_c_made = sem("neg_c_made")
        unit_high_made = sem("unit_high_made")
        unit_low_made = sem("unit_low_made")
        unit_cut_made = sem("unit_cut_made")
        gate_a_made = sem("gate_a_made")
        gate_a_scaled = sem("gate_a_scaled")
        c_taken = sem("c_taken")
        u_made = sem("u_made")
        last_u_kept = sem("last_u_kept")
        conv_made = sem("conv_made")
        z_made = sem("z_made")
        z_squared = sem("z_squared")
        z_squares_added = sem("z_squares_added")
        gate_c_made = sem("gate_c_made")
        z_gated = sem("z_gated")
        z_sums_made = sem("z_sums_made")
        z_rms_made = sem("z_rms_made")
        pads_made = sem("pads_made")
        high_made = sem("high_made")
        low_parts_made = sem("low_parts_made")
        c_cols_made = sem("c_cols_made")
        kq_turned = sem("kq_turned")
        kq_taken_act = sem("kq_taken_act")
        kq_taken_dve = sem("kq_taken_dve")
        scored = sem("scored")
        max_made = sem("max_made")
        exp_made = sem("exp_made")
        p_turned = sem("p_turned")
        p_taken_dve = sem("p_taken_dve")
        p_taken_act = sem("p_taken_act")
        weighed = sem("weighed")
        o_taken = sem("o_taken")
        o_turned = sem("o_turned")
        den_inverted = sem("den_inverted")
        attended = sem("attended")
        wo_high_made = sem("wo_high_made")
        wo_low_made_pool = sem("wo_low_made_pool")
        wo_low_made_dve = sem("wo_low_made_dve")
        wo_block_used = sem("wo_block_used")
        a_squared = sem("a_squared")
        a_rms_made = sem("a_rms_made")
        norms_inverted = sem("norms_inverted")
        z_high_made = sem("z_high_made")
        z_low_made = sem("z_low_made")
        mix_turned = sem("mix_turned")
        mix_made = sem("mix_made")
        mix_high_made = sem("mix_high_made")
        mix_low_made = sem("mix_low_made")
        y_summed = sem("y_summed")
        y_half_made = sem("y_half_made")
        y_made = sem("y_made")

        x_all = [x_prompt[0, i * P:(i + 1) * P, :] for i in range(PB)] + [x_sample[0]]
        k_dst = [k_prompt[0, 0, i * P:(i + 1) * P].rearrange("t h d -> t (h d)") for i in range(PB)] + [
            k_sample[0, 0].rearrange("t h d -> t (h d)")]
        v_dst = [v_prompt[0, 0, i * P:(i + 1) * P].rearrange("t h d -> t (h d)") for i in range(PB)] + [
            v_sample[0, 0].rearrange("t h d -> t (h d)")]
        y_dst = [y_prompt[0, i * P:(i + 1) * P, :] for i in range(PB)] + [y_sample[0]]
        w_rows = w_in[0].rearrange("(k p) n -> p k n", p=P)
        wo_rows = w_out[0].rearrange("(k p) n -> p k n", p=P)

        units = [("a", j, 3 * AD + j * P) for j in range(CJ)]
        for j in range(CJ):
            units += [("C", j, COL_C + j * P), ("h", j, COL_H + j * P), ("B", j, COL_B + j * P), ("g", j, COL_G + j * P)]
        UN = len(units)

        def unit_w(t, u):
            return t[:, (u % 2) * 1024:(u % 2 + 1) * 1024].rearrange("p (k n) -> p k n", k=KD)

        def low_made(c, k):
            return (w_low_made_dve if k % 2 else w_low_made_pool), KD // 2 * c + k // 2 + 1

        def low4_made(n, k):
            if n == 0:
                return wo_low_made_pool, k + 1
            return (wo_low_made_dve, k // 2 + 1) if k % 2 else (wo_low_made_pool, KD + k // 2 + 1)

        block = ctx.enter_context(nc.Block())

        WORDER = [4, 5, 6, 7, 0, 1, 2, 3]
        NCONST = 9

        @block.sync
        def _(sp):
            def load_x(i):
                if i >= 2:
                    sp.wait_ge(h_normed, i - 1)
                sp.dma_start(xt[0:rows(i), i % 2, :], x_all[i]).then_inc(x_loaded[i % 2], 16)

            def load_w(c, k):
                if c:
                    sp.wait_ge(*low_made(c - 1, k))
                sp.dma_start(w_raw[:, k * 512:(k + 1) * 512], w_rows[:, k, c * 512:(c + 1) * 512]).then_inc(w_loaded[k], 16)

            load_x(0)
            sp.dma_start(g_x[:, :], norm_g[0:1, :].to_broadcast([P, DM])).then_inc(first_loaded, 16)
            sp.dma_start(ident[:, :], eye).then_inc(first_loaded, 16)
            load_w(0, 0)
            load_x(1)
            for k in range(1, KD):
                load_w(0, k)
            sp.dma_start(g_q[:, :], q_norm_g[0:1, :].to_broadcast([P, HD])).then_inc(small_loaded, 16)
            sp.dma_start(g_k[:, :], k_norm_g[0:1, :].to_broadcast([P, HD])).then_inc(small_loaded, 16)
            sp.dma_start(g_att[:, :], att_out_g).then_inc(small_loaded, 16)
            sp.dma_start(g_conv[:, :], conv_out_g).then_inc(small_loaded, 16)
            sp.dma_start(taps[:, :, :], conv_w).then_inc(small_loaded, 16)
            sp.dma_start(past_u[:, :, :], state_conv).then_inc(small_loaded, 16)
            sp.dma_start(b_bc[:, :], b_f[0:1, :].to_broadcast([P, NH])).then_inc(small_loaded, 16)
            sp.dma_start(upto_f[:, :], upto).then_inc(small_loaded, 16)
            sp.dma_start(ones_f[:, :], future).then_inc(small_loaded, 16)
            sp.dma_start(wf_raw[:, :, :], w_rows[:, :, COL_F:COL_F + NH]).then_inc(wf_loaded, 16)
            sp.dma_start(lf[:, NEW + 1:NB, :], cache_logf[0, 0].rearrange("(b p) h -> p b h", p=P)).then_inc(cached_lf_loaded, 16)
            for i in range(2, NT):
                load_x(i)
            for k in range(KD):
                load_w(1, k)
            for k in range(KD):
                load_w(2, k)
            for i in range(NT):
                sp.wait_ge(heads_normed, NT + i + 1)
                sp.dma_start(k_dst[i], kn[0:rows(i), i, :]).then_inc(k_stored[i % 2], 16)
            for u in range(UN):
                if u < 2:
                    sp.wait_ge(*low_made(2, KD - 1))
                    sp.wait_ge(*low_made(2, KD - 2))
                else:
                    sp.wait_ge(unit_low_made, u - 1)
                sp.dma_start(unit_w(w_raw, u), w_rows[:, :, units[u][2]:units[u][2] + P]).then_inc(unit_loaded[u % 2], 16)
                if u == 1:
                    for i in range(NT):
                        sp.wait_ge(proj_taken, 2 * NT + i + 1)
                        sp.dma_start(v_dst[i], v_out[0:rows(i), i % 2, :]).then_inc(v_stored[i % 2], 16)
            sp.wait_ge(lf_made, 1)
            sp.dma_start(logf_prompt[0, 0].rearrange("(b p) h -> p b h", p=P), lf[:, 0:PB, :]).then_inc(lf_stored, 16)
            sp.dma_start(logf_sample[0, 0], lf[0:NS, NEW, :]).then_inc(lf_stored, 16)
            sp.wait_ge(last_u_kept, 2 * CJ)
            sp.dma_start(conv_last, last_u[:, :, :]).then_inc(conv_stored, 16)
            sp.wait_ge(v_stored[0], 16 * 5)
            sp.wait_ge(v_stored[1], 16 * 4)
            for h in range(NH):
                if h:
                    sp.wait_ge(low_parts_made, 3 * h - 1)
                sp.dma_start(k_raw[:, :, :], cache_k[0, 0, :, h, :].rearrange("(b p) d -> p b d", p=P)).then_inc(cached_k_loaded, 16)
                if h == 0:
                    sp.wait_ge(unit_cut_made, 3 * UN)
                    sp.wait_ge(z_squares_added, CJ)
                elif h >= 2:
                    sp.wait_ge(weighed, CHUNKS * (h - 1))
                v = v_raw[:, h % 2]
                sp.dma_start(v[:, 0:PB, :], v_prompt[0, 0, :, h, :].rearrange("(b p) d -> p b d", p=P)).then_inc(v_loaded[h % 2], 16)
                sp.dma_start(v[0:NS, NEW, :], v_sample[0, 0, :, h, :]).then_inc(v_loaded[h % 2], 16)
                sp.dma_start(v[:, NEW + 1:NB, :], cache_v[0, 0, :, h, :].rearrange("(b p) d -> p b d", p=P)).then_inc(v_loaded[h % 2], 16)
            def load_wo(n, k):
                b = WORDER[k]
                if n:
                    sp.wait_ge(*low4_made(0, k))
                elif k == 0:
                    sp.wait_ge(scored, NT * (NH - 1))
                sp.dma_start(w4_raw[:, k * 512:(k + 1) * 512], wo_rows[:, b, n * 512:(n + 1) * 512]).then_inc(wo_loaded[k], 16)

            def load_res(e):
                n, i = divmod(e, NT)
                if e >= 2:
                    sp.wait_ge(y_half_made, e - 1)
                sp.dma_start(x_res[0:rows(i), e % 2, :], x_all[i][:, n * 512:(n + 1) * 512]).then_inc(residual_loaded[e % 2], 16)

            def store_y(e):
                n, i = divmod(e, NT)
                sp.wait_ge(y_made, e + 1)
                sp.dma_start(y_dst[i][:, n * 512:(n + 1) * 512], y_out[0:rows(i), e % 2, :]).then_inc(y_stored[e % 2], 16)

            for k in range(KD):
                load_wo(0, k)
            sp.wait_ge(low_parts_made, 3 * NH)
            sp.wait_ge(k_stored[0], 16 * 5)
            sp.wait_ge(k_stored[1], 16 * 4)
            load_res(0)
            load_res(1)
            for k in range(KD):
                load_wo(1, k)
            for e in range(2 * NT):
                if e + 2 < 2 * NT:
                    load_res(e + 2)
                store_y(e)
            sp.wait_ge(y_stored[0], 16 * NT)
            sp.wait_ge(y_stored[1], 16 * NT)
            sp.wait_ge(lf_stored, 32)
            sp.wait_ge(conv_stored, 16)

        @block.scalar
        def _(act):
            def square_x(i):
                r = rows(i)
                act.wait_ge(x_loaded[i % 2], 16 * (i // 2 + 1))
                act.activation(ps[0:r, 4:6, :].rearrange("p b n -> p (b n)"), xt[0:r, i % 2, :], ACT.Square,
                               accum_out=x_ss[0:r, i:i + 1]).then_inc(x_squared, 1)
                act.wait_ge(x_squared, i + 1)
                act.activation(x_rms[0:r, i:i + 1], x_ss[0:r, i:i + 1], ACT.Sqrt, scale=1.0 / DM,
                               bias=eps_c[0:r, :]).then_inc(x_rms_made, 1)

            def w_high(c, k):
                act.wait_ge(w_loaded[k], 16 * (c + 1))
                if c:
                    if k < KD - 1:
                        act.wait_ge(w_block_used, (c - 1) * (KD - 1) + k + 1)
                    else:
                        act.wait_ge(projected, c * NT)
                act.copy(w_hi[:, k * 512:(k + 1) * 512], w_raw[:, k * 512:(k + 1) * 512]).then_inc(w_high_made, 1)

            def h_high(i):
                r = rows(i)
                act.wait_ge(h_turned, i + 1)
                act.copy(h_hi[:, :, i * P:i * P + r],
                         ps[:, 2 * (i % 2):2 * (i % 2) + 2, :].rearrange("p b (k t) -> p (b k) t", t=P)[:, :, 0:r]
                         ).then_inc(h_high_made, 1)

            def evict(c, i):
                r, e = rows(i), c * NT + i
                act.wait_ge(projected, e + 1)
                src = ps[0:r, 6 + e % 2, :]
                if i == NT - 1:
                    act.copy(s_part[:, :], ps[NS:P, 6 + e % 2, :]).then_inc(halves_taken, 1)
                    act.wait_ge(whole_made, c + 1)
                    src = s_whole[:, :]
                if c == 2:
                    if i >= 2:
                        act.wait_ge(v_stored[i % 2], 16 * (i // 2))
                    act.copy(v_out[0:r, i % 2, :], src).then_inc(proj_taken, 1)
                    return
                if e >= 2:
                    act.wait_ge(heads_summed, e - 1)
                act.copy((qn if c == 0 else kn)[0:r, i, :], src)
                act.activation(sq[0:r, e % 2, :], src, ACT.Square).then_inc(proj_taken, 1)

            def root(e):
                r = rows(e % NT)
                act.wait_ge(heads_summed, e + 1)
                act.activation(qk_rms[0:r, e, :], qk_ss[0:r, e, :], ACT.Sqrt, scale=1.0 / HD,
                               bias=eps_c[0:r, :]).then_inc(heads_rooted, 1)

            act.wait_ge(consts_made, 1)
            act.activation(warm[:, :], eps_c[:, :], ACT.Sqrt)
            square_x(0)
            w_high(0, 0)
            h_high(0)
            w_high(0, 1)
            square_x(1)
            for k in range(2, KD):
                w_high(0, k)
            h_high(1)
            square_x(2)
            for i in range(1, NT):
                if i + 1 < NT:
                    h_high(i + 1)
                if i + 2 < NT:
                    square_x(i + 2)
                evict(0, i - 1)
                if i >= 2:
                    root(i - 2)
            for k in range(KD):
                w_high(1, k)
            evict(0, NT - 1)
            root(NT - 2)
            for i in range(NT):
                if i == NT - 1:
                    for k in range(KD):
                        w_high(2, k)
                evict(1, i)
                root(NT + i - 1)
            act.wait_ge(wf_loaded, 16)
            act.copy(wf_sp[:, :, 0:NH], wf_raw[:, :, :]).then_inc(unit_high_made, 1)
            for i in range(NT):
                evict(2, i)
                if i == 0:
                    root(2 * NT - 1)

            def unit_high(u):
                act.wait_ge(unit_loaded[u % 2], 16 * (u // 2 + 1))
                act.wait_ge(projected, 3 * NT)
                if u >= 2:
                    act.wait_ge(unit_cut_made, 3 * (u - 1))
                act.copy(unit_w(w_hi, u), unit_w(w_raw, u)).then_inc(unit_high_made, 1)

            unit_high(0)
            unit_high(1)
            for n, (t0, w) in enumerate(CUTS):
                act.wait_ge(f_logits_made, n + 1)
                act.copy(fT[:, t0:t0 + w], ps[0:2 * NH, n, 0:w]).then_inc(f_logits_taken, 1)
            act.wait_ge(f_step, 2)
            act.activation(f2[:, :, :], f1[:, :, :], ACT.Exp).then_inc(f_step, 1)
            act.wait_ge(f_step, 3)
            act.activation(f3[:, :, :], f2[:, :, :], ACT.Ln, bias=1.0).then_inc(f_step, 1)
            for u, (kind, j, _) in enumerate(units):
                bank = 3 * (u % 2)
                if kind == "C":
                    if j:
                        act.wait_ge(z_gated, j)
                    for n, (t0, w) in enumerate(CUTS):
                        act.wait_ge(unit_cut_made, 3 * u + n + 1)
                        act.copy(c_sb[:, t0:t0 + w], ps[:, bank + n, 0:w]).then_inc(c_taken, 1)
                if kind in "ag":
                    if kind == "g" and j:
                        act.wait_ge(z_gated, j)
                    if kind == "a" and j == 0:
                        act.wait_ge(proj_taken, 3 * NT)
                        act.wait_ge(v_stored[0], 16 * 5)
                        act.wait_ge(v_stored[1], 16 * 4)
                        act.wait_ge(heads_normed, 2 * NT)
                        act.wait_ge(f_step, 1)
                    for n, (t0, w) in enumerate(CUTS):
                        act.wait_ge(unit_cut_made, 3 * u + n + 1)
                        dst = silu_a[:, j, t0:t0 + w] if kind == "a" else g_cv[:, t0:t0 + w]
                        act.activation(dst, ps[:, bank + n, 0:w], ACT.Silu).then_inc(gate_a_made if kind == "a" else gate_c_made, 1)
                if kind == "B":
                    act.wait_ge(z_made, 4 * (j + 1))
                    if j:
                        act.wait_ge(z_squares_added, j)
                    act.activation(z_sq[:, :], z_cv[:, :], ACT.Square).then_inc(z_squared, 1)
                if u + 2 < UN:
                    unit_high(u + 2)
            def split_high(h, piece):
                cols = slice(h * HD, (h + 1) * HD)
                if h == 0 and piece == 0:
                    act.wait_ge(unit_cut_made, 3 * UN)
                elif h and piece == 0:
                    act.wait_ge(kq_turned, GROUPS * h)
                if piece == 0:
                    act.copy(k_sp[:, 0:NT, 1, :], kn[:, :, cols]).then_inc(high_made, 1)
                elif piece == 1:
                    act.wait_ge(cached_k_loaded, 16 * (h + 1))
                    act.copy(k_sp[:, NT:NB, 1, :], k_raw[:, :, :]).then_inc(high_made, 1)
                else:
                    act.copy(q_sp[:, :, 0:2, :], qn[:, :, cols].unsqueeze(2).to_broadcast([P, NT, 2, HD])).then_inc(high_made, 1)

            def spread(h, g):
                if not by_dve(h, g):
                    act.wait_ge(kq_turned, GROUPS * h + g + 1)
                    if g < 3 and h >= 2:
                        act.wait_ge(scored, NT * (h - 1))
                    act.copy(kqT[:, h % 2, 4 * g:4 * g + 4, :], bank_kq(h, g)).then_inc(kq_taken_act, 1)

            def soft(h, i):
                act.wait_ge(max_made, NT * h + i + 1)
                if h or i >= 2:
                    act.wait_ge(p_turned, T_HEAD * h + T_BEFORE[i - 1] if i else T_HEAD * (h - 1) + T_BEFORE[NT - 1])
                r, nk = item_shape(i)
                n = (NT * h + i) % 2
                act.activation(prob[0:r, n, 0:nk], scores(i)[0:r, 0:nk], ACT.Exp,
                               bias=neg_max[0:r, n:n + 1], accum_out=den[0:r, h % 2, i:i + 1]).then_inc(exp_made, 1)

            def t_second(h, i):
                c = i // 2
                act.wait_ge(p_turned, T_HEAD * h + T_BEFORE[i] + 2)
                if i % 2 == 0:
                    act.wait_ge(weighed, CHUNKS * h + c - 1)
                act.copy(t_dst(i, 1), t_src(i, 1)).then_inc(p_taken_act, 1)

            def o_take(h, c):
                w = 2 * P if c < 4 else NS
                act.wait_ge(weighed, CHUNKS * h + c + 1)
                if h or c:
                    act.wait_ge(o_turned, CHUNKS * h + c)
                act.copy(o_sum[:, 0:w], ps[0:HD, 7, 0:w]).then_inc(o_taken, 1)

            def o_put(h, c):
                i0, i1 = (2 * c, 2 * c + 2) if c < 4 else (PB, NT)
                m = rows(i0)
                act.wait_ge(den_inverted, CHUNKS * h + c + 1)
                act.wait_ge(o_turned, CHUNKS * h + c + 1)
                for i in range(i0, i1):
                    ins = act.activation(qn[0:m, i, h * HD:(h + 1) * HD], ps[0:m, 7, 256 + (i - i0) * HD:256 + (i - i0 + 1) * HD],
                                         ACT.Copy, scale=rden[0:m, h % 2, i:i + 1])
                ins.then_inc(attended, 1)

            def wo_high(n, k):
                act.wait_ge(wo_loaded[k], 16 * (n + 1))
                if n == 0:
                    act.wait_ge(kq_turned, GROUPS * NH)
                elif k < KD - 1:
                    act.wait_ge(wo_block_used, k + 1)
                else:
                    act.wait_ge(y_summed, NT)
                act.copy(w4_hi[:, k * 512:(k + 1) * 512], w4_raw[:, k * 512:(k + 1) * 512]).then_inc(wo_high_made, 1)

            for piece in range(3):
                split_high(0, piece)
            act.activation(warm[:, :], eps_c[:, :], ACT.Exp)
            for g in range(GROUPS):
                spread(0, g)
            act.wait_ge(z_gated, CJ)
            act.wait_ge(z_squares_added, CJ)
            soft(0, 0)
            for s in range(STEPS + 1):
                h, i = divmod(s, NT)
                ahead = kq_at(i) if s < STEPS and h + 1 < NH else []
                for g in ahead if i else ():
                    spread(h + 1, g)
                for c_h, c in puts_at(s):
                    o_put(c_h, c)
                if s < STEPS and i in T_SECOND and i % 2:
                    t_second(h, i)
                if s < STEPS and i == 7 and h + 2 < NH:
                    split_high(h + 2, 0)
                if s + 1 < STEPS:
                    soft(*divmod(s + 1, NT))
                for g in ahead if i == 0 else ():
                    spread(h + 1, g)
                for c_h, c in takes_at(s):
                    o_take(c_h, c)
                if s < STEPS and i in T_SECOND and i % 2 == 0:
                    t_second(h, i)
                if s < STEPS and i == 7 and h + 2 < NH:
                    split_high(h + 2, 1)
                elif i == 2 and h and h + 1 < NH:
                    split_high(h + 1, 2)
                if h == NH - 1 and i < KD:
                    wo_high(0, i)
            o_put(NH - 1, 4)

            act.wait_ge(attended, CHUNKS * NH)

            def z_high(i):
                r = rows(i)
                act.copy(m_hi[:, CJ:KD, i * P:i * P + r], zg[:, :, i * P:i * P + r]).then_inc(z_high_made, 1)

            def mix_high(i):
                r = rows(i)
                act.wait_ge(mix_made, i + 1)
                act.copy(m_hi[:, 0:CJ, i * P:i * P + r],
                         mix_f[:, i % 2, :].rearrange("p (j t) -> p j t", j=CJ)[:, :, 0:r]).then_inc(mix_high_made, 1)

            z_high(0)
            mix_high(0)
            act.wait_ge(z_sums_made, 1)
            act.activation(z_rms[:, 0:PB], ps[:, 6, 0:2 * PB:2], ACT.Sqrt, scale=1.0 / CD, bias=eps_c[:, :]).then_inc(z_rms_made, 1)
            act.activation(z_rms[0:NS, PB:NT], ps[0:NS, 6, 2 * PB:2 * PB + 1], ACT.Sqrt, scale=1.0 / CD,
                           bias=eps_c[0:NS, :]).then_inc(z_rms_made, 1)
            for i in range(NT):
                r = rows(i)
                act.activation(a_sq[0:r, :], qn[0:r, i, :], ACT.Square, accum_out=a_ss[0:r, i:i + 1]).then_inc(a_squared, 1)
                act.wait_ge(a_squared, i + 1)
                act.activation(a_rms[0:r, i:i + 1], a_ss[0:r, i:i + 1], ACT.Sqrt, scale=1.0 / AD, bias=eps_c[0:r, :]).then_inc(a_rms_made, 1)
                if i == NT - 1:
                    break
                z_high(i + 1)
                mix_high(i + 1)
            for k in range(KD):
                wo_high(1, k)

        @block.gpsimd
        def _(pool):
            for c in range(3):
                for k in range(0, KD, 2):
                    b = slice(k * 512, (k + 1) * 512)
                    pool.wait_ge(w_high_made, c * KD + k + 1)
                    pool.tensor_tensor(w_lo[:, b], w_raw[:, b], w_hi[:, b].bitcast(F32), ALU.subtract).then_inc(w_low_made_pool, 1)
            pool.wait_ge(unit_high_made, 1)
            pool.tensor_tensor(wf_sp[:, :, NH:2 * NH], wf_raw[:, :, :], wf_sp[:, :, 0:NH].bitcast(F32), ALU.subtract).then_inc(wf_split, 1)
            with pool.Fori(0, UN, 2) as u:
                for n in range(2):
                    pool.wait_ge(unit_high_made, u + (n + 2))
                    pool.tensor_tensor(unit_w(w_lo, n), unit_w(w_raw, n), unit_w(w_hi, n).bitcast(F32), ALU.subtract).then_inc(unit_low_made, 1)
            with pool.Fori(0, NH) as h:
                cols = bass.ds(h * HD, HD)
                pool.wait_ge(high_made, h * 3 + 1)
                pool.tensor_tensor(k_sp[:, 0:NT, 0, :], kn[:, :, cols], k_sp[:, 0:NT, 1, :].bitcast(F32), ALU.subtract).then_inc(low_parts_made, 1)
                pool.wait_ge(high_made, h * 3 + 2)
                pool.tensor_tensor(k_sp[:, NT:NB, 0, :], k_raw[:, :, :], k_sp[:, NT:NB, 1, :].bitcast(F32), ALU.subtract).then_inc(low_parts_made, 1)
                pool.wait_ge(high_made, h * 3 + 3)
                pool.tensor_tensor(q_sp[:, :, 2, :], qn[:, :, cols], q_sp[:, :, 0, :].bitcast(F32), ALU.subtract).then_inc(low_parts_made, 1)
            for n in range(2):
                for k in range(0, KD, n + 1):
                    b = slice(k * 512, (k + 1) * 512)
                    pool.wait_ge(wo_high_made, n * KD + k + 1)
                    pool.tensor_tensor(w4_lo[:, b], w4_raw[:, b], w4_hi[:, b].bitcast(F32), ALU.subtract).then_inc(wo_low_made_pool, 1)

        @block.vector
        def _(dve):
            done = [0]

            def link(ins):
                done[0] += 1
                ins.then_inc(dve_chain, 1)
                dve.wait_ge(dve_chain, done[0])

            dve.memset(eps_c[:, :], EPS).then_inc(consts_made, 1)
            dve.memset(qn[NS:P, PB, :], 0.0)
            dve.memset(kn[NS:P, PB, :], 0.0)
            dve.memset(lf[:, NEW, :], 0.0)
            dve.memset(fx[:, :, :], 0.0)

            def normalise(i):
                r = rows(i)
                dve.wait_ge(x_rms_made, i + 1)
                link(dve.reciprocal(x_inv[0:r, i:i + 1], x_rms[0:r, i:i + 1]))
                if i >= 2:
                    dve.wait_ge(h_turned, i - 1)
                dve.scalar_tensor_tensor(out=hn[0:r, i % 2, :], in0=xt[0:r, i % 2, :], scalar=x_inv[0:r, i:i + 1],
                                         in1=g_x[0:r, :], op0=ALU.mult, op1=ALU.mult).then_inc(h_normed, 1)

            def h_low(i):
                r = rows(i)
                dve.wait_ge(h_high_made, i + 1)
                cols = slice(i * P, i * P + r)
                dve.tensor_tensor(h_lo[:, :, cols],
                                  ps[:, 2 * (i % 2):2 * (i % 2) + 2, :].rearrange("p b (k t) -> p (b k) t", t=P)[:, :, 0:r],
                                  h_hi[:, :, cols].bitcast(F32), ALU.subtract).then_inc(h_low_made, 1)

            def add_halves(c):
                if c:
                    dve.wait_ge(proj_taken, NT * c)
                dve.wait_ge(halves_taken, c + 1)
                dve.tensor_tensor(s_whole[:, :], ps[0:NS, 6 + (c * NT + NT - 1) % 2, :], s_part[:, :], ALU.add).then_inc(whole_made, 1)

            def sums(e):
                r = rows(e % NT)
                dve.wait_ge(proj_taken, e + 1)
                dve.tensor_reduce(qk_ss[0:r, e, :], sq[0:r, e % 2, :].rearrange("p (h d) -> p h d", h=NH), AX,
                                  ALU.add).then_inc(heads_summed, 1)

            def norm(e):
                c, i = divmod(e, NT)
                r = rows(i)
                t, g = (qn, g_q) if c == 0 else (kn, g_k)
                v = t[0:r, i, :].rearrange("p (h d) -> p h d", h=NH)
                dve.wait_ge(heads_rooted, e + 1)
                link(dve.reciprocal(qk_inv[0:r, e, :], qk_rms[0:r, e, :]))
                if c == 0:
                    link(dve.tensor_scalar(qk_inv[0:r, e, :], qk_inv[0:r, e, :], HD ** -0.5, None, ALU.mult))
                link(dve.tensor_tensor(v, v, qk_inv[0:r, e, :].unsqueeze(2).to_broadcast([r, NH, HD]), ALU.mult))
                dve.tensor_tensor(v, v, g[0:r, :].unsqueeze(1).to_broadcast([r, NH, HD]), ALU.mult).then_inc(heads_normed, 1)

            dve.wait_ge(first_loaded, 32)
            def w_low(c, k):
                b = slice(k * 512, (k + 1) * 512)
                dve.wait_ge(w_high_made, c * KD + k + 1)
                dve.tensor_tensor(w_lo[:, b], w_raw[:, b], w_hi[:, b].bitcast(F32), ALU.subtract).then_inc(w_low_made_dve, 1)

            normalise(0)
            h_low(0)
            w_low(0, 1)
            normalise(1)
            w_low(0, 3)
            w_low(0, 5)
            w_low(0, 7)
            h_low(1)
            normalise(2)
            for i in range(1, NT):
                if i + 1 < NT:
                    h_low(i + 1)
                if i + 2 == NT:
                    dve.wait_ge(h_low_made, NT)
                    dve.tensor_copy(h_s[:, :, 0, :], h_hi[:, :, SEQ:TOK].bitcast(F32))
                    dve.tensor_copy(h_s[:, :, 1, :], h_lo[:, :, SEQ:TOK].bitcast(F32)).then_inc(sample_split, 1)
                if i + 2 < NT:
                    normalise(i + 2)
                if i == 1:
                    dve.wait_ge(small_loaded, 16 * NCONST)
                    dve.tensor_copy(ident_r[:, :], ident[:, :]).then_inc(consts_made, 1)
                    dve.tensor_copy(ident_b[:, :], ident[:, :]).then_inc(consts_made, 1)
                    link(dve.tensor_copy(future_b[:, :], ones_f[:, :]))
                    dve.memset(ones_f[:, :], 1.0).then_inc(consts_made, 1)
                sums(i - 1)
                if i >= 2:
                    norm(i - 2)
            for e in range(NT - 1, 2 * NT):
                if e in (NT - 1, 2 * NT - 1):
                    for k in range(1, KD, 2):
                        w_low(e // NT + 1, k)
                    add_halves(e // NT)
                sums(e)
                norm(e - 1)
            norm(2 * NT - 1)
            add_halves(2)

            dve.wait_ge(f_step, 1)
            dve.tensor_copy(f4[:, 0:PB, :], ps[:, 6, 0:2 * PB * NH].rearrange("p (b s h) -> p b s h", s=2, h=NH)[:, :, 1, :])\
               .then_inc(dve_chain, 1)
            link(dve.tensor_copy(f4[0:NS, PB, :], ps[0:NS, 6, (2 * PB + 1) * NH:2 * NT * NH]))
            done[0] += 1
            dve.wait_ge(dve_chain, done[0])
            dve.tensor_tensor(fx[:, 0:PB, :], ps[:, 6, 0:2 * PB * NH].rearrange("p (b s h) -> p b s h", s=2, h=NH)[:, :, 0, :],
                              f4[:, 0:PB, :], ALU.add).then_inc(dve_chain, 1)
            link(dve.tensor_tensor(fx[0:NS, PB, :], ps[0:NS, 6, 2 * PB * NH:(2 * PB + 1) * NH], f4[0:NS, PB, :], ALU.add))
            done[0] += 1
            dve.wait_ge(dve_chain, done[0])
            link(dve.tensor_tensor(fx[:, :, :], fx[:, :, :], b_bc[:, :].unsqueeze(1).to_broadcast([P, NT, NH]), ALU.add))
            link(dve.tensor_scalar(f2[:, :, :], fx[:, :, :], -1.0, None, ALU.mult))
            dve.tensor_tensor(f1[:, :, :], fx[:, :, :], f2[:, :, :], ALU.min).then_inc(f_step, 1)
            dve.wait_ge(f_step, 4)
            link(dve.tensor_scalar(f4[:, :, :], f2[:, :, :], 1.0, None, ALU.add))
            link(dve.reciprocal(f1[:, :, :], f4[:, :, :]))
            link(dve.tensor_scalar(f4[:, :, :], f4[:, :, :], -1.0, None, ALU.add))
            link(dve.tensor_tensor(f4[:, :, :], f2[:, :, :], f4[:, :, :], ALU.subtract))
            link(dve.tensor_tensor(f4[:, :, :], f4[:, :, :], f1[:, :, :], ALU.mult))
            link(dve.tensor_tensor(f3[:, :, :], f3[:, :, :], f4[:, :, :], ALU.add))
            dve.scalar_tensor_tensor(out=lf[:, 0:NT, :], in0=fx[:, :, :], scalar=0.0, in1=f3[:, :, :], op0=ALU.min,
                                     op1=ALU.subtract).then_inc(lf_made, 1)
            dve.wait_ge(sums_made, 2)
            link(dve.tensor_copy(total[:, :, :], ps[:, 6, NB * NH:2 * NB * NH].rearrange("p (b h) -> p b h", h=NH)))
            dve.memset(before[:, 0, :], 0.0).then_inc(dve_chain, 1)
            done[0] += 1
            link(dve.memset(before[:, NEW + 1, :], 0.0))
            for b in range(1, PB):
                dve.tensor_tensor(before[:, b, :], before[:, b - 1, :], total[:, b - 1, :], ALU.add).then_inc(dve_chain, 1)
                done[0] += 1
                link(dve.tensor_tensor(before[:, NEW + 1 + b, :], before[:, NEW + b, :], total[:, NEW + b, :], ALU.add))
            link(dve.tensor_tensor(before[:, NEW, :], before[:, NB - 1, :], total[:, NB - 1, :], ALU.add))
            link(dve.scalar_tensor_tensor(out=neg_c[:, :, :], in0=ps[:, 6, 0:NB * NH].rearrange("p (b h) -> p b h", h=NH),
                                          scalar=-1.0, in1=before[:, :, :], op0=ALU.mult, op1=ALU.subtract))
            link(dve.tensor_copy(neg_c2[:, :, :, 0], neg_c[:, :, :]))
            dve.tensor_tensor(neg_c2[:, :, :, 1], neg_c[:, :, :], neg_c2[:, :, :, 0].bitcast(F32), ALU.subtract).then_inc(neg_c_made, 1)
            for j in range(CJ):
                dve.wait_ge(gate_a_made, 3 * (j + 1))
                dve.tensor_scalar(silu_a[:, j, :], silu_a[:, j, :], g_att[:, j:j + 1], None, ALU.mult).then_inc(gate_a_scaled, 1)
            def c_cols(h):
                if h:
                    dve.wait_ge(kq_turned, GROUPS * h)
                else:
                    dve.wait_ge(pads_made, 3)
                    dve.wait_ge(neg_c_made, 1)
                dve.tensor_copy(k_sp[:, :, 2, 0:2], neg_c2[:, :, h, :].bitcast(F32)).then_inc(c_cols_made, 1)

            link(dve.memset(u_cv[:, 0:2], 0.0))
            for u, (kind, j, _) in enumerate(units):
                bank = 3 * (u % 2)
                if kind == "h":
                    if j:
                        dve.wait_ge(conv_made, j)
                    dve.tensor_copy(u_cv[:, SEQ + 2:SEQ + 4], past_u[:, j, :]).then_inc(u_made, 1)
                    for n, (t0, w) in enumerate(CUTS):
                        dve.wait_ge(unit_cut_made, 3 * u + n + 1)
                        dve.wait_ge(c_taken, 3 * j + n + 1)
                        if n < 2:
                            dve.tensor_tensor(u_cv[:, 2 + t0:2 + t0 + w], ps[:, bank + n, 0:w], c_sb[:, t0:t0 + w],
                                              ALU.mult).then_inc(u_made, 1)
                        else:
                            m = SEQ - t0
                            dve.tensor_tensor(u_cv[:, 2 + t0:2 + SEQ], ps[:, bank + n, 0:m], c_sb[:, t0:SEQ], ALU.mult)\
                               .then_inc(u_made, 1)
                            dve.tensor_tensor(u_cv[:, SEQ + 4:SEQ + 4 + NS], ps[:, bank + n, m:w], c_sb[:, SEQ:TOK],
                                              ALU.mult).then_inc(u_made, 1)
                    dve.wait_ge(u_made, 5 * (j + 1))
                    W = TOK + 2
                    dve.tensor_copy(last_u[:, j, 0:2], u_cv[:, SEQ:SEQ + 2]).then_inc(last_u_kept, 1)
                    dve.tensor_copy(last_u[:, j, 2:4], u_cv[:, TOK + 2:TOK + 4]).then_inc(last_u_kept, 1)
                    link(dve.tensor_scalar(y_cv[:, :], u_cv[:, 0:W], taps[:, j, 0:1], None, ALU.mult))
                    link(dve.scalar_tensor_tensor(out=y_cv[:, :], in0=u_cv[:, 1:W + 1], scalar=taps[:, j, 1:2],
                                                  in1=y_cv[:, :], op0=ALU.mult, op1=ALU.add))
                    dve.scalar_tensor_tensor(out=y_cv[:, :], in0=u_cv[:, 2:W + 2], scalar=taps[:, j, 2:3],
                                             in1=y_cv[:, :], op0=ALU.mult, op1=ALU.add).then_inc(conv_made, 1)
                if kind == "B":
                    dve.wait_ge(conv_made, j + 1)
                    if j:
                        dve.wait_ge(z_squared, j)
                        dve.wait_ge(z_gated, j)
                    for n, (t0, w) in enumerate(CUTS):
                        dve.wait_ge(unit_cut_made, 3 * u + n + 1)
                        m = min(w, SEQ - t0)
                        ins = dve.tensor_tensor(z_cv[:, t0:t0 + m], ps[:, bank + n, 0:m], y_cv[:, t0:t0 + m], ALU.mult)
                        if m < w:
                            ins.then_inc(z_made, 1)
                            ins = dve.tensor_tensor(z_cv[:, SEQ:TOK], ps[:, bank + n, m:w], y_cv[:, SEQ + 2:TOK + 2], ALU.mult)
                        ins.then_inc(z_made, 1)
                if u == UN - 1:
                    dve.wait_ge(unit_cut_made, 3 * UN)
                    dve.memset(k_sp[:, :, 2, :].bitcast(F32), 0.0).then_inc(pads_made, 1)
                    dve.memset(q_sp[:, :, 3, 2:HD].bitcast(F32), 0.0).then_inc(pads_made, 1)
                    dve.memset(q_sp[:, :, 3, 0:2].bitcast(F32), 1.0).then_inc(pads_made, 1)
                    c_cols(0)
                if kind == "g":
                    dve.wait_ge(gate_c_made, 3 * (j + 1))
                    dve.wait_ge(z_made, 4 * (j + 1))
                    dve.scalar_tensor_tensor(out=zg[:, j, :], in0=z_cv[:, :], scalar=g_conv[:, j:j + 1], in1=g_cv[:, :],
                                             op0=ALU.mult, op1=ALU.mult).then_inc(z_gated, 1)
                    dve.wait_ge(z_squared, j + 1)
                    if j == 0:
                        dve.tensor_copy(z_ss[:, :], z_sq[:, :]).then_inc(z_squares_added, 1)
                    else:
                        dve.wait_ge(z_squares_added, j)
                        dve.tensor_tensor(z_ss[:, :], z_ss[:, :], z_sq[:, :], ALU.add).then_inc(z_squares_added, 1)

            def spread(h, g):
                if by_dve(h, g):
                    dve.wait_ge(kq_turned, GROUPS * h + g + 1)
                    if g < 3 and h >= 2:
                        dve.wait_ge(scored, NT * (h - 1))
                    dve.tensor_copy(kqT[:, h % 2, 4 * g:4 * g + 4, :], bank_kq(h, g)).then_inc(kq_taken_dve, 1)

            def top(h, i):
                dve.wait_ge(scored, NT * h + i + 1)
                if h or i >= 2:
                    dve.wait_ge(exp_made, NT * h + i - 1)
                r, nk = item_shape(i)
                n = (NT * h + i) % 2
                dve.tensor_reduce(neg_max[0:r, n:n + 1], scores(i)[0:r, 0:nk], AX, ALU.max, negate=True).then_inc(max_made, 1)

            def t_first(h, i):
                c = i // 2
                dve.wait_ge(p_turned, T_HEAD * h + T_BEFORE[i] + 1)
                if i % 2 == 0 and c >= 2:
                    dve.wait_ge(weighed, CHUNKS * h + c - 1)
                elif i == 0 and h:
                    dve.wait_ge(weighed, CHUNKS * h)
                dve.tensor_copy(t_dst(i, 0), t_src(i, 0)).then_inc(p_taken_dve, 1)

            def den_invert(h, c):
                i0, i1 = (2 * c, 2 * c + 2) if c < 4 else (PB, NT)
                m = rows(i0)
                dve.wait_ge(exp_made, NT * h + i1)
                if h >= 2:
                    dve.wait_ge(attended, CHUNKS * (h - 1))
                dve.reciprocal(rden[0:m, h % 2, i0:i1], den[0:m, h % 2, i0:i1]).then_inc(den_inverted, 1)

            for g in range(GROUPS):
                spread(0, g)
            top(0, 0)
            c_cols(1)
            cols = slice(HD, 2 * HD)
            dve.tensor_copy(k_sp[:, 0:NT, 1, :], kn[:, :, cols]).then_inc(high_made, 1)
            dve.wait_ge(cached_k_loaded, 16 * 2)
            dve.tensor_copy(k_sp[:, NT:NB, 1, :], k_raw[:, :, :]).then_inc(high_made, 1)
            dve.tensor_copy(q_sp[:, :, 0:2, :], qn[:, :, cols].unsqueeze(2).to_broadcast([P, NT, 2, HD])).then_inc(high_made, 1)
            for s in range(STEPS + 1):
                h, i = divmod(s, NT)
                ahead = kq_at(i) if s < STEPS and h + 1 < NH else []
                if i == 7:
                    t_first(h, i)
                for g in ahead if i == 0 else ():
                    spread(h + 1, g)
                if s + 1 < STEPS:
                    top(*divmod(s + 1, NT))
                for c_h, c in takes_at(s):
                    den_invert(c_h, c)
                if s < STEPS and i in KQ_LATE:
                    t_first(h, i)
                for g in ahead if i else ():
                    spread(h + 1, g)
                if s < STEPS and i not in KQ_LATE and i != 7:
                    t_first(h, i)
                if s < STEPS and i == 7 and h + 2 < NH:
                    c_cols(h + 2)

            def z_low(i):
                cols = slice(i * P, i * P + rows(i))
                dve.wait_ge(z_high_made, i + 1)
                dve.tensor_tensor(m_lo[:, CJ:KD, cols], zg[:, :, cols], m_hi[:, CJ:KD, cols].bitcast(F32), ALU.subtract).then_inc(z_low_made, 1)

            def mix(i):
                r = rows(i)
                cols = slice(i * P, i * P + r)
                m = mix_f[:, i % 2, :].rearrange("p (j t) -> p j t", j=CJ)[:, :, 0:r]
                dve.wait_ge(mix_turned, i + 1)
                dve.tensor_tensor(m, ps[:, i % 2, :].rearrange("p (j t) -> p j t", j=CJ)[:, :, 0:r], silu_a[:, :, cols],
                                  ALU.mult).then_inc(mix_made, 1)

            def mix_low(i):
                r = rows(i)
                cols = slice(i * P, i * P + r)
                m = mix_f[:, i % 2, :].rearrange("p (j t) -> p j t", j=CJ)[:, :, 0:r]
                dve.wait_ge(mix_high_made, i + 1)
                dve.tensor_tensor(m_lo[:, 0:CJ, cols], m, m_hi[:, 0:CJ, cols].bitcast(F32), ALU.subtract).then_inc(mix_low_made, 1)

            def wo_low(k):
                b = slice(k * 512, (k + 1) * 512)
                dve.wait_ge(wo_high_made, KD + k + 1)
                dve.tensor_tensor(w4_lo[:, b], w4_raw[:, b], w4_hi[:, b].bitcast(F32), ALU.subtract).then_inc(wo_low_made_dve, 1)

            def result(e):
                n, i = divmod(e, NT)
                r = rows(i)
                bank = 2 + 2 * (e % 3)
                if n == 0:
                    dve.wait_ge(a_rms_made, i + 1)
                    dve.reciprocal(a_inv[0:r, i:i + 1], a_rms[0:r, i:i + 1]).then_inc(norms_inverted, 1)
                    dve.wait_ge(norms_inverted, 3 + i)
                dve.wait_ge(y_summed, e + 1)
                dve.wait_ge(residual_loaded[e % 2], 16 * (e // 2 + 1))
                if e:
                    dve.wait_ge(y_made, e)
                dve.scalar_tensor_tensor(out=y_part[0:r, :], in0=ps[0:r, bank, :], scalar=z_inv[0:r, i:i + 1],
                                         in1=x_res[0:r, e % 2, :], op0=ALU.mult, op1=ALU.add).then_inc(y_half_made, 1)
                dve.wait_ge(y_half_made, e + 1)
                if e >= 2:
                    dve.wait_ge(y_stored[e % 2], 16 * (e // 2))
                dve.scalar_tensor_tensor(out=y_out[0:r, e % 2, :], in0=ps[0:r, bank + 1, :], scalar=a_inv[0:r, i:i + 1],
                                         in1=y_part[0:r, :], op0=ALU.mult, op1=ALU.add).then_inc(y_made, 1)

            z_low(0)
            mix(0)
            mix_low(0)
            dve.wait_ge(z_rms_made, 2)
            dve.reciprocal(z_inv[:, 0:PB], z_rms[:, 0:PB]).then_inc(norms_inverted, 1)
            dve.reciprocal(z_inv[0:NS, PB:NT], z_rms[0:NS, PB:NT]).then_inc(norms_inverted, 1)
            for i in range(1, NT):
                z_low(i)
                mix(i)
                mix_low(i)
                result(i - 1)
            for k in range(1, KD, 2):
                wo_low(k)
            for e in range(NT - 1, 2 * NT):
                result(e)

        @block.tensor
        def _(pe):
            def three(out, a_hi, a_lo, b_hi, b_lo, first, last):
                pe.matmul(out, a_hi, b_hi, start=first, stop=False)
                pe.matmul(out, a_hi, b_lo, start=False, stop=False)
                return pe.matmul(out, a_lo, b_hi, start=False, stop=last)

            def turn_x(i):
                r = rows(i)
                pe.wait_ge(h_normed, i + 1)
                if i >= 2:
                    pe.wait_ge(h_low_made, i - 1)
                for k in range(KD):
                    t = pe.transpose(ps[:, 2 * (i % 2) + k // 4, (k % 4) * P:(k % 4) * P + r],
                                     hn[0:r, i % 2, k * P:(k + 1) * P], ident[0:r, 0:r])
                t.then_inc(h_turned, 1)

            def project(c, i):
                e, r = c * NT + i, rows(i)
                if e >= 2:
                    pe.wait_ge(proj_taken, e - 1)
                if c == 0:
                    pe.wait_ge(h_low_made, i + 1)
                    if i == NT - 1:
                        pe.wait_ge(sample_split, 1)
                cols = slice(i * P, i * P + r)
                for k in range(KD):
                    if i == 0:
                        pe.wait_ge(*low_made(c, k))
                    w = slice(k * 512, (k + 1) * 512)
                    if i < PB:
                        m = three(ps[0:r, 6 + e % 2, :], h_hi[:, k, cols], h_lo[:, k, cols], w_hi[:, w], w_lo[:, w], k == 0, k == KD - 1)
                    else:
                        both = h_s[:, k].rearrange("p s t -> p (s t)")
                        pe.matmul(ps[:, 6 + e % 2, :], both, w_hi[:, w], start=k == 0, stop=False)
                        m = pe.matmul(ps[:, 6 + e % 2, :], both, w_lo[:, w], start=False, stop=k == KD - 1)
                    if e == 0 and k == 1:
                        turn_x(1)
                    if i == NT - 1 and k < KD - 1:
                        m.then_inc(w_block_used, 1)
                m.then_inc(projected, 1)

            pe.wait_ge(first_loaded, 32)
            turn_x(0)
            for c in range(3):
                for i in range(NT):
                    if c == 0 and i + 1 < NT and i:
                        turn_x(i + 1)
                    project(c, i)
            pe.wait_ge(wf_split, 1)
            for n, (t0, w) in enumerate(CUTS):
                if n == 0:
                    pe.wait_ge(h_low_made, NT)
                for k in range(KD):
                    pe.matmul(ps[0:2 * NH, n, 0:w], wf_sp[:, k, :], h_hi[:, k, t0:t0 + w], start=k == 0, stop=False)
                    m = pe.matmul(ps[0:2 * NH, n, 0:w], wf_sp[:, k, :], h_lo[:, k, t0:t0 + w], start=False, stop=k == KD - 1)
                m.then_inc(f_logits_made, 1)
            pe.wait_ge(f_logits_taken, 3)
            pe.wait_ge(proj_taken, 3 * NT)
            for i in range(NT):
                t = pe.transpose(ps[0:rows(i), 6, i * 2 * NH:(i + 1) * 2 * NH], fT[:, i * P:i * P + rows(i)],
                                 ident[0:2 * NH, 0:2 * NH])
            t.then_inc(f_step, 1)

            def cumulate():
                pe.wait_ge(lf_made, 1)
                pe.wait_ge(cached_lf_loaded, 16)
                pe.matmul(ps[:, 6, 0:NB * NH], upto_f[:, :], lf[:, :, :], start=True, stop=True).then_inc(sums_made, 1)
                pe.matmul(ps[:, 6, NB * NH:2 * NB * NH], ones_f[:, :], lf[:, :, :], start=True, stop=True).then_inc(sums_made, 1)

            for u, (kind, j, _) in enumerate(units):
                bank = 3 * (u % 2)
                if u == 0:
                    pe.wait_ge(f_logits_taken, 3)
                if u >= 2:
                    k2, j2, _ = units[u - 2]
                    if k2 == "a":
                        pe.wait_ge(gate_a_made, 3 * (j2 + 1))
                    elif k2 == "C":
                        pe.wait_ge(c_taken, 3 * (j2 + 1))
                    elif k2 == "h":
                        pe.wait_ge(u_made, 5 * (j2 + 1))
                    elif k2 == "B":
                        pe.wait_ge(z_made, 4 * (j2 + 1))
                    else:
                        pe.wait_ge(gate_c_made, 3 * (j2 + 1))
                pe.wait_ge(unit_low_made, u + 1)
                wh, wl = unit_w(w_hi, u), unit_w(w_lo, u)
                for n, (t0, w) in enumerate(CUTS):
                    for k in range(KD):
                        m = three(ps[:, bank + n, 0:w], wh[:, k, :], wl[:, k, :], h_hi[:, k, t0:t0 + w], h_lo[:, k, t0:t0 + w],
                                  k == 0, k == KD - 1)
                    m.then_inc(unit_cut_made, 1)
                if u == 1:
                    cumulate()
            def kq_group(h, g):
                if g == 0:
                    pe.wait_ge(low_parts_made, 3 * h + 1)
                    pe.wait_ge(c_cols_made, h + 1)
                elif g == NT * 2 // 4:
                    pe.wait_ge(low_parts_made, 3 * h + 2)
                elif g == NB * 2 // 4:
                    pe.wait_ge(low_parts_made, 3 * h + 3)
                if h == 0:
                    if g >= len(KQ_FIRST):
                        pe.wait_ge(*kq_read(0, g - len(KQ_FIRST)))
                else:
                    pe.wait_ge(*(kq_read(h, g - 1) if g else kq_read(h - 1, GROUPS - 1)))
                for n in range(4):
                    b, part = divmod(4 * g + n, 2)
                    if b < NB:
                        src = k_sp[:, b, part:part + 2, :]
                    else:
                        src = q_sp[:, b - NB, 2 * part:2 * part + 2, :]
                    t = pe.transpose(ps_r[:, kq_bank(h, g), n * P:(n + 1) * P], src.rearrange("p s d -> p (s d)"), ident_r[:, :])
                t.then_inc(kq_turned, 1)

            def score(h, i):
                if i == 0:
                    for mine in (False, True):
                        pe.wait_ge(*kq_read(h, max(g for g in range(GROUPS) if by_dve(h, g) == mine)))
                if i == 0 and h:
                    pe.wait_ge(exp_made, NT * h - 2)
                elif i == 1 and h:
                    pe.wait_ge(exp_made, NT * h)
                elif i >= 2:
                    pe.wait_ge(exp_made, NT * h + (i if i == 8 else i - 1))
                m = rows(i)
                out = scores(i)
                if i < PB:
                    pieces = [(b, min(b + 4, i + 1), b * P) for b in range(0, i + 1, 4)]
                else:
                    pieces = [(NT, NT + 4, 0), (NT + 4, NB, 512), (NEW, NEW + 1, PAST)]
                par = kqT[:, h % 2].rearrange("p (b s) n -> p b s n", s=2)
                for b0, b1, col in pieces:
                    width = P if b0 != NEW or i < PB else NS
                    own = b1 == i + 1 if i < PB else b0 == NEW
                    n = (b1 - b0) * width
                    for part in range(2):
                        ins = pe.matmul(out[0:m, col:col + n], par[:, NB + i, part, 0:m], par[:, b0:b1, part, 0:width],
                                        start=part == 0, stop=part == 1 and not own)
                    if own:
                        ins = pe.matmul(out[0:m, col + n - width:col + n], ident_b[0:m, 0:m], future_b[0:m, 0:width],
                                        start=False, stop=True)
                ins.then_inc(scored, 1)

            def turn_p(h, i):
                pe.wait_ge(exp_made, NT * h + i + 1)
                m = rows(i)
                for g, blocks in enumerate(T_GROUPS[i]):
                    n = T_BEFORE[i] + g
                    if n >= 2:
                        pe.wait_ge(*p_read(h, *T_LIST[n - 2]))
                    elif h:
                        pe.wait_ge(*p_read(h - 1, *T_LIST[n - 2]))
                    for b in blocks:
                        w = P if b < 8 else NS
                        t = pe.transpose(ps[0:w, 4 + n % 2, (b - blocks[0]) * m:(b - blocks[0] + 1) * m],
                                         prob[0:m, (NT * h + i) % 2, b * P:b * P + w], ident[0:m, 0:m])
                    t.then_inc(p_turned, 1)

            def weigh(h, c):
                if c == 0:
                    pe.wait_ge(v_loaded[h % 2], 48 * (h // 2 + 1))
                if h or c:
                    pe.wait_ge(attended, CHUNKS * h + c)
                last = 2 * c + 1 if c < 4 else PB
                pe.wait_ge(*p_read(h, last, 0))
                t, v = pT[:, c % 2, :], v_raw[:, h % 2]
                if c < 4:
                    for b in range(2 * c + 2):
                        if b == 4:
                            pe.wait_ge(*p_read(h, last, 1))
                        q0 = 0 if b <= 2 * c else P
                        ins = pe.matmul(ps[0:HD, 7, q0:256], v[:, b, :], t[:, b * 256 + q0:(b + 1) * 256], start=b == 0,
                                        stop=b == 2 * c + 1, skip_group_check=True)
                else:
                    for n in range(9):
                        k = P if n < 8 else NS
                        b = NT + n if n < 8 else NEW
                        if n == 8:
                            pe.wait_ge(*p_read(h, PB, 1))
                        ins = pe.matmul(ps[0:HD, 7, 0:NS], v[0:k, b, :], t[0:k, n * NS:(n + 1) * NS], start=n == 0,
                                        stop=n == 8, skip_group_check=True)
                ins.then_inc(weighed, 1)

            def o_turn(h, c):
                pe.wait_ge(o_taken, CHUNKS * h + c + 1)
                if h or c:
                    pe.wait_ge(attended, CHUNKS * h + c)
                for n in range(2 if c < 4 else 1):
                    m = P if c < 4 else NS
                    t = pe.transpose(ps[0:m, 7, 256 + n * HD:256 + (n + 1) * HD], o_sum[:, n * P:n * P + m], ident[0:HD, 0:HD])
                t.then_inc(o_turned, 1)

            for g in range(GROUPS):
                kq_group(0, g)
            score(0, 0)
            for s in range(STEPS + 1):
                h, i = divmod(s, NT)
                ahead = kq_at(i) if s < STEPS and h + 1 < NH else []
                if s + 1 < STEPS:
                    score(*divmod(s + 1, NT))
                for g in ahead[0:1]:
                    kq_group(h + 1, g)
                for c_h, c in puts_at(s):
                    o_turn(c_h, c)
                if s < STEPS and i in KQ_LATE:
                    turn_p(h, i)
                for g in ahead[1:] if i == 0 else ():
                    kq_group(h + 1, g)
                for c_h, c in takes_at(s):
                    weigh(c_h, c)
                for g in ahead[1:] if i else ():
                    kq_group(h + 1, g)
                if s == STEPS - 1:
                    pe.wait_ge(z_squares_added, CJ)
                    for n in range(NT):
                        r = rows(n)
                        m = pe.matmul(ps[0:r, 6, 2 * n:2 * n + 2], z_ss[:, n * P:n * P + r], ones_f[:, 0:2], start=True, stop=True)
                    m.then_inc(z_sums_made, 1)
                if s < STEPS and i not in KQ_LATE:
                    turn_p(h, i)
            o_turn(NH - 1, 4)

            def turn_mix(i):
                r = rows(i)
                if i == 0:
                    pe.wait_ge(attended, CHUNKS * NH)
                if i >= 2:
                    pe.wait_ge(mix_made, i - 1)
                for j in range(CJ):
                    t = pe.transpose(ps[:, i % 2, j * P:j * P + r], qn[0:r, i, j * P:(j + 1) * P], ident[0:r, 0:r])
                t.then_inc(mix_turned, 1)

            turn_mix(0)
            for e in range(2 * NT):
                n, i = divmod(e, NT)
                r = rows(i)
                bank = 2 + 2 * (e % 3)
                cols = slice(i * P, i * P + r)
                if n == 0 and i + 1 < NT:
                    turn_mix(i + 1)
                if e >= 3:
                    pe.wait_ge(y_made, e - 2)
                for k in range(KD):
                    if i == 0:
                        pe.wait_ge(*low4_made(n, k))
                    if n == 0 and k == 0:
                        pe.wait_ge(z_low_made, i + 1)
                    if n == 0 and k == 4:
                        pe.wait_ge(mix_low_made, i + 1)
                    w = slice(k * 512, (k + 1) * 512)
                    m = three(ps[0:r, bank + k // 4, :], m_hi[:, WORDER[k], cols], m_lo[:, WORDER[k], cols], w4_hi[:, w], w4_lo[:, w],
                              k % 4 == 0, k % 4 == 3)
                    if n == 0 and i == NT - 1 and k < KD - 1:
                        m.then_inc(wo_block_used, 1)
                    if k == KD - 1:
                        m.then_inc(y_summed, 1)
    return nc


_OUTS = [("y_prompt", (1, SEQ, DM)), ("y_sample", (1, NS, DM)), ("k_prompt", (1, 1, SEQ, NH, HD)),
         ("v_prompt", (1, 1, SEQ, NH, HD)), ("logf_prompt", (1, 1, SEQ, NH)), ("k_sample", (1, 1, NS, NH, HD)),
         ("v_sample", (1, 1, NS, NH, HD)), ("logf_sample", (1, 1, NS, NH)), ("conv_last", (P, CJ, 4))]


def kernel(**inputs):
    import numpy as np
    import concourse.bacc as bacc
    from concourse.bass_utils import run_bass_kernel_spmd

    def by_channel(a):
        return np.ascontiguousarray(a.reshape(-1, CJ, P).transpose(2, 1, 0))

    a = {n: np.asarray(v) for n, v in inputs.items()}
    for n in ("state_conv", "conv_w"):
        a[n] = by_channel(a[n].reshape(-1, CD))
    for n in ("att_out_g", "conv_out_g"):
        a[n] = by_channel(a[n])[:, :, 0]
    q = np.arange(P)
    a["eye"] = np.eye(P, dtype=np.float32)
    a["future"] = np.where(q[None, :] > q[:, None], np.float32(-1e30), np.float32(0))
    a["upto"] = (q[:, None] <= q[None, :]).astype(np.float32)
    nc = bacc.Bacc("TRN2", target_bir_lowering=False, num_devices=1)
    arrays, args = {}, {}
    for n, v in a.items():
        v = np.ascontiguousarray(v)
        arrays[f"in_{n}"] = v
        args[n] = nc.dram_tensor(f"in_{n}", v.shape, F32, kind="ExternalInput").ap()
    for n, shape in _OUTS:
        args[n] = nc.dram_tensor(f"out_{n}", shape, F32, kind="ExternalOutput").ap()
    build(nc, **args)
    r = run_bass_kernel_spmd(nc, [arrays], core_ids=[0]).results[0]
    last = np.asarray(r["out_conv_last"]).transpose(2, 1, 0).reshape(4, CD)
    return (r["out_y_prompt"], r["out_y_sample"], r["out_k_prompt"], r["out_v_prompt"], r["out_logf_prompt"],
            last[0:2].reshape(1, 1, 2, CD), r["out_k_sample"], r["out_v_sample"], r["out_logf_sample"],
            last[2:4].reshape(1, 1, 2, CD))
```
